# Optimizing a Trainium2 kernel written in Bass

```python
import jax, jax.numpy as jnp
from jax import lax
import numpy as np
import math

D_MODEL = 1024
BATCH = 1
SEQ = 256
DEPTH = 1

N_HEADS = 8
HEAD_DIM = 64
ATTN_WIDTH = N_HEADS * HEAD_DIM
IDX_HEADS = 8
IDX_DIM = 64
TOPK_MAX = 256
Q_BLOCK = 128
CONV_CH = 512
CONV_WIDTH = 31
D_FF = -(-8 * D_MODEL // (3 * 256)) * 256
N_MOD = 6
EPS = 1e-6


def _in_split_sizes():
    return [ATTN_WIDTH, ATTN_WIDTH, ATTN_WIDTH,
            IDX_HEADS * IDX_DIM, IDX_DIM, IDX_HEADS,
            2 * CONV_CH, D_MODEL, D_MODEL]

def rmsnorm(x, g):
    xf = x.astype(jnp.float32)
    y = xf * lax.rsqrt(jnp.mean(xf * xf, axis=-1, keepdims=True) + EPS) * g.astype(jnp.float32)
    return y.astype(x.dtype)

def layernorm(x, g, b):
    xf = x.astype(jnp.float32)
    mu = jnp.mean(xf, axis=-1, keepdims=True)
    var = jnp.mean(jnp.square(xf - mu), axis=-1, keepdims=True)
    y = (xf - mu) * lax.rsqrt(var + EPS) * g.astype(jnp.float32) + b.astype(jnp.float32)
    return y.astype(x.dtype)

def modulate(h, shift, scale):
    return h * (1.0 + scale[:, None, :]) + shift[:, None, :]

def dsa_attention(q, k, v, q_idx, k_idx, w_idx):
    B, S = q.shape[0], q.shape[1]
    topk = min(TOPK_MAX, S // 4)
    n_blocks = S // Q_BLOCK
    f32 = jnp.float32
    slopes = jnp.exp2(-8.0 * jnp.arange(1, N_HEADS + 1, dtype=f32) / N_HEADS)
    key_pos = jnp.arange(S)
    k_idx32 = k_idx.astype(f32)
    gather = jax.vmap(lambda arr, ix: arr[ix])

    def one_block(i):
        start = i * Q_BLOCK
        qb = lax.dynamic_slice_in_dim(q, start, Q_BLOCK, axis=1).astype(f32)
        qib = lax.dynamic_slice_in_dim(q_idx, start, Q_BLOCK, axis=1).astype(f32)
        wb = lax.dynamic_slice_in_dim(w_idx, start, Q_BLOCK, axis=1).astype(f32)
        q_pos = start + jnp.arange(Q_BLOCK)
        idx_logits = jnp.einsum('btjd,bsd->btjs', qib, k_idx32) * (IDX_DIM ** -0.5)
        score = jnp.einsum('btj,btjs->bts', wb, jax.nn.relu(idx_logits))
        causal = key_pos[None, :] <= q_pos[:, None]
        score = jnp.where(causal[None], score, -jnp.inf)
        _, sel = lax.top_k(score, topk)
        k_sel = gather(k, sel).astype(f32)
        v_sel = gather(v, sel).astype(f32)
        s = jnp.einsum('bthd,btkhd->bhtk', qb, k_sel) * (HEAD_DIM ** -0.5)
        dist = (q_pos[None, :, None] - sel).astype(f32)
        s = s - slopes[None, :, None, None] * dist[:, None]
        valid = sel <= q_pos[None, :, None]
        s = jnp.where(valid[:, None], s, -jnp.inf)
        p = jax.nn.softmax(s, axis=-1)
        out = jnp.einsum('bhtk,btkhd->bthd', p, v_sel)
        return out.astype(q.dtype)

    outs = lax.map(one_block, jnp.arange(n_blocks))
    return jnp.transpose(outs, (1, 0, 2, 3, 4)).reshape(B, S, N_HEADS * HEAD_DIM)

def conformer_conv(u, w_dw, b_dw, ln_g, ln_b):
    a, g = jnp.split(u, 2, axis=-1)
    z = a * jax.nn.sigmoid(g)
    z = lax.conv_general_dilated(z, w_dw, window_strides=(1,), padding=[(CONV_WIDTH - 1, 0)],
                                 dimension_numbers=('NWC', 'WIO', 'NWC'),
                                 feature_group_count=CONV_CH) + b_dw
    z = layernorm(z, ln_g, ln_b)
    return jax.nn.silu(z)

def first_inputs(seed: int = 0) -> dict:
    key = jax.random.key(seed)
    ks = jax.random.split(key, 20)
    n_in = sum(_in_split_sizes())

    def nrm(k, shape, fan_in, gain=1.0):
        return jax.random.normal(k, shape, jnp.float32) * (gain * fan_in ** -0.5)

    def gain_vec(k, shape):
        return 1.0 + 0.02 * jax.random.normal(k, shape, jnp.float32)

    def small(k, shape):
        return 0.02 * jax.random.normal(k, shape, jnp.float32)

    return {
        "x": jax.random.normal(ks[0], (BATCH, SEQ, D_MODEL), jnp.float32),
        "c": jax.random.normal(ks[1], (BATCH, D_MODEL), jnp.float32),
        "norm_mix_g": gain_vec(ks[2], (DEPTH, D_MODEL)),
        "w_in": nrm(ks[3], (DEPTH, D_MODEL, n_in), D_MODEL),
        "w_dw": nrm(ks[4], (DEPTH, CONV_WIDTH, 1, CONV_CH), CONV_WIDTH),
        "b_dw": small(ks[5], (DEPTH, CONV_CH)),
        "conv_ln_g": gain_vec(ks[6], (DEPTH, CONV_CH)),
        "conv_ln_b": small(ks[7], (DEPTH, CONV_CH)),
        "w_attn_proj": nrm(ks[8], (DEPTH, ATTN_WIDTH, D_MODEL), ATTN_WIDTH),
        "w_conv_proj": nrm(ks[9], (DEPTH, CONV_CH, D_MODEL), CONV_CH),
        "w_out": nrm(ks[10], (DEPTH, D_MODEL, D_MODEL), D_MODEL),
        "norm_ffn_g": gain_vec(ks[11], (DEPTH, D_MODEL)),
        "w_ffn_in": nrm(ks[12], (DEPTH, D_MODEL, 2 * D_FF), D_MODEL),
        "w_ffn_out": nrm(ks[13], (DEPTH, D_FF, D_MODEL), D_FF),
        "w_ada": nrm(ks[14], (DEPTH, D_MODEL, N_MOD * D_MODEL), D_MODEL, 0.5),
        "b_ada": small(ks[15], (DEPTH, N_MOD * D_MODEL)),
        "norm_final_g": gain_vec(ks[16], (D_MODEL,)),
    }

def first_block(x, c, norm_mix_g, w_in, w_dw, b_dw, conv_ln_g, conv_ln_b, w_attn_proj,
              w_conv_proj, w_out, norm_ffn_g, w_ffn_in, w_ffn_out, w_ada, b_ada, norm_final_g):
    B, S, _ = x.shape
    split_at = list(np.cumsum(_in_split_sizes())[:-1])
    c_act = jax.nn.silu(c)
    for l in range(DEPTH):
        mod = c_act @ w_ada[l] + b_ada[l]
        sh_m, sc_m, g_m, sh_f, sc_f, g_f = jnp.split(mod, N_MOD, axis=-1)

        h = modulate(rmsnorm(x, norm_mix_g[l]), sh_m, sc_m)
        proj = h @ w_in[l]
        q, k, v, qi, ki, wi, u, ga, gb = jnp.split(proj, split_at, axis=-1)
        q = q.reshape(B, S, N_HEADS, HEAD_DIM)
        k = k.reshape(B, S, N_HEADS, HEAD_DIM)
        v = v.reshape(B, S, N_HEADS, HEAD_DIM)
        qi = qi.reshape(B, S, IDX_HEADS, IDX_DIM)
        wi = wi * (IDX_HEADS ** -0.5)
        y_attn = dsa_attention(q, k, v, qi, ki, wi) @ w_attn_proj[l]
        y_conv = conformer_conv(u, w_dw[l], b_dw[l], conv_ln_g[l], conv_ln_b[l]) @ w_conv_proj[l]
        merged = jax.nn.sigmoid(ga) * y_attn + jax.nn.sigmoid(gb) * y_conv
        x = x + g_m[:, None, :] * (merged @ w_out[l])

        h = modulate(rmsnorm(x, norm_ffn_g[l]), sh_f, sc_f)
        a, b = jnp.split(h @ w_ffn_in[l], 2, axis=-1)
        x = x + g_f[:, None, :] * ((jax.nn.silu(a) * b) @ w_ffn_out[l])
    return rmsnorm(x, norm_final_g)


CHUNK = 64
N_MEM = 256
ROPE_THETA = 10000.0
NEG = -1e30

A_HEADS = 4
A_DK = 64
A_DV = 2 * A_DK
A_QK_W = A_HEADS * 2 * A_DK
A_WIDTH = A_HEADS * A_DV

B_HEADS = 8
B_DH = 64
B_WIDTH = B_HEADS * B_DH
B_LEFT_CHUNKS = 8
B_MAX_REL = 256

X_HEADS = 4
X_DH = D_MODEL // X_HEADS

D_FF_2 = -(-(8 * D_MODEL) // (3 * 256)) * 256

OFF_QA = 0
OFF_KA = OFF_QA + A_QK_W
OFF_VA = OFF_KA + A_QK_W
OFF_QB = OFF_VA + A_WIDTH
OFF_KB = OFF_QB + B_WIDTH
OFF_VB = OFF_KB + B_WIDTH
OFF_GA = OFF_VB + B_WIDTH
OFF_GB = OFF_GA + D_MODEL
IN_COLS = OFF_GB + D_MODEL


def rmsnorm_2(x, g):
    xf = x.astype(jnp.float32)
    y = xf * lax.rsqrt(jnp.mean(xf * xf, axis=-1, keepdims=True) + EPS)
    return (y * g.astype(jnp.float32)).astype(x.dtype)

def rope_tables(seq, dim):
    inv = 1.0 / (ROPE_THETA ** (jnp.arange(0, dim, 2, dtype=jnp.float32) / dim))
    ang = jnp.arange(seq, dtype=jnp.float32)[:, None] * inv[None, :]
    return jnp.cos(ang), jnp.sin(ang)

def apply_rope(x, cos, sin):
    x1, x2 = jnp.split(x.astype(jnp.float32), 2, axis=-1)
    out = jnp.concatenate([x1 * cos - x2 * sin, x2 * cos + x1 * sin], axis=-1)
    return out.astype(x.dtype)

def diff_attention(q, k, v, lam, subln_g, lam_init):
    b, s = q.shape[0], q.shape[1]
    nqb = s // Q_BLOCK
    scale = A_DK ** -0.5
    k_chunk = jnp.arange(s) // CHUNK
    qb = q.reshape(b, nqb, Q_BLOCK, A_HEADS, 2, A_DK).transpose(1, 0, 2, 3, 4, 5)

    def one_block(args):
        qi, blk = args
        sc = jnp.einsum('bqhcd,bkhcd->bchqk', qi, k).astype(jnp.float32) * scale
        q_chunk = (blk * Q_BLOCK + jnp.arange(Q_BLOCK)) // CHUNK
        mask = k_chunk[None, :] <= q_chunk[:, None]
        sc = jnp.where(mask[None, None, None], sc, NEG)
        p = jax.nn.softmax(sc, axis=-1)
        attn = p[:, 0] - lam * p[:, 1]
        return jnp.einsum('bhqk,bkhd->bqhd', attn.astype(v.dtype), v)

    o = lax.map(one_block, (qb, jnp.arange(nqb)))
    o = o.transpose(1, 0, 2, 3, 4).reshape(b, s, A_HEADS, A_DV)
    o = rmsnorm_2(o, subln_g) * (1.0 - lam_init)
    return o.reshape(b, s, A_WIDTH)

def chunk_band_attention(q, k, v, rel_bias):
    b, s = q.shape[0], q.shape[1]
    nc = s // CHUNK
    pad = B_LEFT_CHUNKS * CHUNK
    band = pad + CHUNK
    scale = B_DH ** -0.5
    kp = jnp.pad(k, ((0, 0), (pad, 0), (0, 0), (0, 0)))
    vp = jnp.pad(v, ((0, 0), (pad, 0), (0, 0), (0, 0)))
    i = jnp.arange(CHUNK)
    j = jnp.arange(band)
    dist = i[:, None] + pad - j[None, :]
    idx = jnp.clip(dist, -B_MAX_REL, B_MAX_REL) + B_MAX_REL
    bias = rel_bias[:, idx].astype(jnp.float32)
    qc = q.reshape(b, nc, CHUNK, B_HEADS, B_DH).transpose(1, 0, 2, 3, 4)

    def one_chunk(args):
        qi, c = args
        start = c * CHUNK
        kb = lax.dynamic_slice_in_dim(kp, start, band, axis=1)
        vb = lax.dynamic_slice_in_dim(vp, start, band, axis=1)
        sc = jnp.einsum('bqhd,bkhd->bhqk', qi, kb).astype(jnp.float32) * scale + bias[None]
        valid = (start + j) >= pad
        sc = jnp.where(valid[None, None, None, :], sc, NEG)
        p = jax.nn.softmax(sc, axis=-1)
        return jnp.einsum('bhqk,bkhd->bqhd', p.astype(vb.dtype), vb)

    o = lax.map(one_chunk, (qc, jnp.arange(nc)))
    return o.transpose(1, 0, 2, 3, 4).reshape(b, s, B_WIDTH)

def memory_cross_attention(h, m, w_cq, w_ckv, w_co):
    b, s = h.shape[0], h.shape[1]
    nm = m.shape[1]
    q = (h @ w_cq).reshape(b, s, X_HEADS, X_DH)
    k, v = jnp.split(m @ w_ckv, 2, axis=-1)
    k = k.reshape(b, nm, X_HEADS, X_DH)
    v = v.reshape(b, nm, X_HEADS, X_DH)
    sc = jnp.einsum('bshd,bmhd->bhsm', q, k).astype(jnp.float32) * (X_DH ** -0.5)
    p = jax.nn.softmax(sc, axis=-1)
    o = jnp.einsum('bhsm,bmhd->bshd', p.astype(v.dtype), v).reshape(b, s, D_MODEL)
    return o @ w_co

def swiglu(h, w_gate_up, w_down):
    g, u = jnp.split(h @ w_gate_up, 2, axis=-1)
    return (jax.nn.silu(g) * u) @ w_down

def second_inputs(seed: int = 0) -> dict:
    key = jax.random.key(seed)
    ks = jax.random.split(key, 24)
    nrm = lambda k, shape, sc: jax.random.normal(k, shape, jnp.float32) * sc
    gain = lambda k, shape: 1.0 + 0.05 * jax.random.normal(k, shape, jnp.float32)
    L = DEPTH
    return {
        "x": nrm(ks[0], (BATCH, SEQ, D_MODEL), 1.0),
        "mem": nrm(ks[1], (BATCH, N_MEM, D_MODEL), 1.0),
        "norm_mix_g": gain(ks[2], (L, D_MODEL)),
        "w_in": nrm(ks[3], (L, D_MODEL, IN_COLS), D_MODEL ** -0.5),
        "lam_q1": nrm(ks[4], (L, A_DK), 0.1),
        "lam_k1": nrm(ks[5], (L, A_DK), 0.1),
        "lam_q2": nrm(ks[6], (L, A_DK), 0.1),
        "lam_k2": nrm(ks[7], (L, A_DK), 0.1),
        "subln_g": gain(ks[8], (L, A_DV)),
        "rel_bias": nrm(ks[9], (L, B_HEADS, 2 * B_MAX_REL + 1), 0.1),
        "w_up_a": nrm(ks[10], (L, A_WIDTH, D_MODEL), A_WIDTH ** -0.5),
        "w_up_b": nrm(ks[11], (L, B_WIDTH, D_MODEL), B_WIDTH ** -0.5),
        "w_out": nrm(ks[12], (L, D_MODEL, D_MODEL), D_MODEL ** -0.5),
        "norm_cross_g": gain(ks[13], (L, D_MODEL)),
        "norm_mem_g": gain(ks[14], (L, D_MODEL)),
        "w_cq": nrm(ks[15], (L, D_MODEL, D_MODEL), D_MODEL ** -0.5),
        "w_ckv": nrm(ks[16], (L, D_MODEL, 2 * D_MODEL), D_MODEL ** -0.5),
        "w_co": nrm(ks[17], (L, D_MODEL, D_MODEL), D_MODEL ** -0.5),
        "norm_ffn_g": gain(ks[18], (L, D_MODEL)),
        "w_gate_up": nrm(ks[19], (L, D_MODEL, 2 * D_FF_2), D_MODEL ** -0.5),
        "w_down": nrm(ks[20], (L, D_FF_2, D_MODEL), D_FF_2 ** -0.5),
        "norm_final_g": gain(ks[21], (D_MODEL,)),
    }

def second_block(x, mem, norm_mix_g, w_in, lam_q1, lam_k1, lam_q2, lam_k2, subln_g,
              rel_bias, w_up_a, w_up_b, w_out, norm_cross_g, norm_mem_g, w_cq,
              w_ckv, w_co, norm_ffn_g, w_gate_up, w_down, norm_final_g):
    b, s = x.shape[0], x.shape[1]
    cos, sin = rope_tables(s, A_DK)
    cos_a = cos[None, :, None, None, :]
    sin_a = sin[None, :, None, None, :]
    for layer in range(DEPTH):
        lam_init = 0.8 - 0.6 * math.exp(-0.3 * layer)
        h = rmsnorm_2(x, norm_mix_g[layer])
        z = h @ w_in[layer]
        qa = z[..., OFF_QA:OFF_KA].reshape(b, s, A_HEADS, 2, A_DK)
        ka = z[..., OFF_KA:OFF_VA].reshape(b, s, A_HEADS, 2, A_DK)
        va = z[..., OFF_VA:OFF_QB].reshape(b, s, A_HEADS, A_DV)
        qb = z[..., OFF_QB:OFF_KB].reshape(b, s, B_HEADS, B_DH)
        kb = z[..., OFF_KB:OFF_VB].reshape(b, s, B_HEADS, B_DH)
        vb = z[..., OFF_VB:OFF_GA].reshape(b, s, B_HEADS, B_DH)
        ga = z[..., OFF_GA:OFF_GB]
        gb = z[..., OFF_GB:IN_COLS]
        qa = apply_rope(qa, cos_a, sin_a)
        ka = apply_rope(ka, cos_a, sin_a)
        lam = (jnp.exp(jnp.sum(lam_q1[layer].astype(jnp.float32) * lam_k1[layer].astype(jnp.float32)))
               - jnp.exp(jnp.sum(lam_q2[layer].astype(jnp.float32) * lam_k2[layer].astype(jnp.float32)))
               + lam_init)
        ya = diff_attention(qa, ka, va, lam, subln_g[layer], lam_init)
        yb = chunk_band_attention(qb, kb, vb, rel_bias[layer])
        merged = (jax.nn.sigmoid(ga) * (ya @ w_up_a[layer])
                  + jax.nn.sigmoid(gb) * (yb @ w_up_b[layer]))
        x = x + merged @ w_out[layer]
        hc = rmsnorm_2(x, norm_cross_g[layer])
        mn = rmsnorm_2(mem, norm_mem_g[layer])
        x = x + memory_cross_attention(hc, mn, w_cq[layer], w_ckv[layer], w_co[layer])
        hf = rmsnorm_2(x, norm_ffn_g[layer])
        x = x + swiglu(hf, w_gate_up[layer], w_down[layer])
    return rmsnorm_2(x, norm_final_g)


def setup_inputs(seed=0):
    out = dict(first_inputs(seed))
    for name, value in second_inputs(seed + 1).items():
        if name != "x":
            out[name + "_2"] = value
    return out


def reference(
    x, c, norm_mix_g, w_in, w_dw, b_dw, conv_ln_g, conv_ln_b, w_attn_proj, w_conv_proj, w_out,
    norm_ffn_g, w_ffn_in, w_ffn_out, w_ada, b_ada, norm_final_g, mem_2, norm_mix_g_2, w_in_2,
    lam_q1_2, lam_k1_2, lam_q2_2, lam_k2_2, subln_g_2, rel_bias_2, w_up_a_2, w_up_b_2, w_out_2,
    norm_cross_g_2, norm_mem_g_2, w_cq_2, w_ckv_2, w_co_2, norm_ffn_g_2, w_gate_up_2, w_down_2,
    norm_final_g_2,
):
    x = first_block(
        x, c, norm_mix_g, w_in, w_dw, b_dw, conv_ln_g, conv_ln_b, w_attn_proj, w_conv_proj,
        w_out, norm_ffn_g, w_ffn_in, w_ffn_out, w_ada, b_ada, norm_final_g,
    )
    return second_block(
        x, mem_2, norm_mix_g_2, w_in_2, lam_q1_2, lam_k1_2, lam_q2_2, lam_k2_2, subln_g_2,
        rel_bias_2, w_up_a_2, w_up_b_2, w_out_2, norm_cross_g_2, norm_mem_g_2, w_cq_2, w_ckv_2,
        w_co_2, norm_ffn_g_2, w_gate_up_2, w_down_2, norm_final_g_2,
    )


_drawn_inputs = setup_inputs


def setup_inputs(seed=0):
    import zlib

    import numpy as np

    out = dict(_drawn_inputs(seed))
    spreads = {}
    factors = {'norm_mix_g': 4.509,
     'b_dw': 6.16,
     'conv_ln_g': 8.0,
     'conv_ln_b': 8.0,
     'norm_ffn_g': 7.095,
     'lam_q1_2': 8.0,
     'lam_k1_2': 3.133,
     'rel_bias_2': 7.682,
     'norm_cross_g_2': 8.0,
     'norm_mem_g_2': 7.19,
     'lam_q2_2': 3.784,
     'lam_k2_2': 2.764,
     'norm_ffn_g_2': 8.0}
    for name, (base, spread) in spreads.items():
        noise = np.random.default_rng([zlib.crc32(name.encode()), seed]).standard_normal(out[name].shape)
        drawn = base * np.exp(spread * noise) if base else spread * noise
        out[name] = __import__('jax').numpy.asarray(drawn.astype(out[name].dtype))
    for name, factor in factors.items():
        out[name] = (out[name] * factor).astype(out[name].dtype)
    return out
```

```python
from contextlib import ExitStack

import concourse.bass as bass
from concourse import mybir
from concourse.alu_op_type import AluOpType as ALU

F32 = mybir.dt.float32
F32R = mybir.dt.float32r
ACT = mybir.ActivationFunctionType
AX_X = mybir.AxisListType.X

P = 128
SEQ = 256
TT = SEQ // P
D = 1024
KD = D // P
W = 512
DFF = 2816
KF = DFF // P
GW = 256
NSLAB_FF = DFF // GW
EPS = 1e-6
HEADS, DH = 8, 64
TOPK = 64
TAPS = 31
PAD = TAPS - 1
CG = 4
NEG = -1e38
TAKEN = -3e38
BLK = 2048
PIECE = 1024
RAW = 4
RING = 4
IN1 = 5192
IN2 = 5120
C_Q, C_K, C_V, C_QI, C_KI, C_WI, C_U, C_GA, C_GB = 0, 512, 1024, 1536, 2048, 2112, 2120, 3144, 4168
E_QA, E_KA, E_VA, E_QB, E_KB, E_VB, E_GA, E_GB = 0, 512, 1024, 1536, 2048, 2560, 3072, 4096
SMALL = C_U - C_KI


def constants(np):
    parts = {}
    i = np.arange(P)
    parts["ident"] = np.eye(P)
    parts["ones"] = np.ones((P, P))
    parts["mean512"] = np.full((P, P), 1.0 / 512)
    rel = i[None, :] - i[:, None]
    parts["rel"] = np.concatenate([rel - P, rel], 1) * 8.0
    parts["causal"] = np.concatenate([np.zeros((P, P)), np.where(rel <= 0, 0.0, NEG)], 1)
    late = (i[None, :] // 64) > (i[:, None] // 64)
    parts["chunk"] = np.concatenate([np.zeros((P, P)), np.where(late, -8e30, 0.0)], 1)
    inv = 1.0 / (10000.0 ** (np.arange(0, 64, 2, dtype=np.float32) / np.float32(64)))
    ang = np.arange(SEQ, dtype=np.float32)[:, None] * inv.astype(np.float32)[None, :]
    cos, sin = np.cos(ang).astype(np.float32), np.sin(ang).astype(np.float32)
    parts["cos"] = np.concatenate([cos, cos], 1).reshape(TT, P, 64).transpose(1, 0, 2).reshape(P, TT * 64)
    parts["sin"] = np.concatenate([-sin, sin], 1).reshape(TT, P, 64).transpose(1, 0, 2).reshape(P, TT * 64)
    parts["half"] = np.full((P, SEQ), -0.5)
    at, n = {}, 0
    for name, a in parts.items():
        at[name] = (n, n + a.shape[1])
        n += a.shape[1]
    return np.ascontiguousarray(np.concatenate(list(parts.values()), 1).astype(np.float32)), at


P_CKV, U_CKV = 0, 0
P_SMALL, U_SMALL = 16, 4
P_IN1, U_IN1 = 17, 5
P_PA, U_PA = 57, 15
P_PC, U_PC = 61, 17
P_OUT1, U_OUT1 = 65, 19
P_FI1, U_FI1 = 73, 21
P_FO1, U_FO1 = 117, 21
P_IN2, U_IN2 = 139, 23
P_UA, U_UA = 179, 33
P_UB, U_UB = 183, 35
P_OUT2, U_OUT2 = 187, 37
P_CQ, U_CQ = 195, 39
P_CO, U_CO = 203, 41
P_FI2, U_FI2 = 211, 43
P_FO2, U_FO2 = 255, 43
P_END = 277
B_END = 9 + (P_END - 17) // 2


def block_of(p):
    if p < 16:
        return p // 2, p % 2
    if p == 16:
        return 8, 0
    return 9 + (p - 17) // 2, (p - 17) % 2


def pair_blocks(b):
    pairs = [q for p in (P_FI1, P_FI2) for q in range(block_of(p)[0], block_of(p)[0] + 2 * NSLAB_FF + 2)]
    return sum(q <= b and q % RAW == b % RAW for q in pairs) if b in pairs else 0


def last_piece_of(b):
    return 2 * b + 1 if b < 8 else 16 if b == 8 else 17 + 2 * (b - 9) + 1


N_MEM, N_H1, N_H2, N_FINAL1, N_M2, N_CR, N_F2, N_FINAL2 = range(8)
F_OF = {N_MEM: 0, N_H1: 1, N_H2: 2, N_M2: 3, N_CR: 4, N_F2: 5}
V_C, V_MIX, V_FFN, V_MIX2, V_CROSS, V_MEM, V_FFN2, V_CLG, V_CLB, V_BDW, V_SUB, V_ADA = \
    0, 8, 16, 24, 32, 40, 48, 56, 60, 64, 68, 69
V_ROWS = V_ADA + 48


def build(nc, a, out):
    import numpy as np

    table, cols = constants(np)
    const_dram = nc.inline_tensor(table, name="shape_constants")

    cursor = [16512]

    def region(nbytes):
        at = cursor[0]
        cursor[0] += (nbytes + 31) // 32 * 32
        return at

    def sb(name, shape, dtype=F32, at=None):
        n = 4
        for s in shape[1:]:
            n *= s
        return nc.alloc_sbuf_tensor_at(name, shape, dtype, offset=region(n) if at is None else at)

    raw = sb("raw_weights", [P, RAW, BLK])
    w_hi = sb("w_hi", [P, RING, PIECE], F32R)
    w_lo = sb("w_lo", [P, RING, PIECE], F32R)
    a_hi = sb("a_hi", [P, KD, SEQ], F32R)
    a_lo = sb("a_lo", [P, KD, SEQ], F32R)
    x = sb("x_residual", [P, TT, D])
    z_at = region(2 * KF * SEQ * 4)
    z = sb("z_projected", [P, TT, IN1], at=z_at)
    xs_z = sb("scaled_rows_early", [P, TT, D], at=z_at)
    f_z = sb("feature_rows_early", [P, KD, SEQ], at=z_at + 8192)
    mem_rows = sb("mem_rows", [P, TT, D], at=z_at + 16384)
    k_rows = sb("mem_key_rows", [P, TT, D], at=z_at + 24576)
    f_hi = sb("ff_hi", [P, KF, SEQ], F32R, at=z_at)
    f_lo = sb("ff_lo", [P, KF, SEQ], F32R, at=z_at + KF * SEQ * 4)
    mem_kT = sb("mem_kT", [P, KD, SEQ])
    mem_v = sb("mem_v", [P, TT, D])
    g_mix = sb("gate_mix_rows", [P, D])
    g_ffn = sb("gate_ffn_rows", [P, D])
    final_g = sb("final_gain_rows", [P, D])
    const = sb("constants", [P, table.shape[1]])

    def C(name, lo=0, hi=None):
        c0, c1 = cols[name]
        return const[:, c0 + lo:(c1 if hi is None else c0 + hi)]

    ident, ones, mean512 = C("ident"), C("ones"), C("mean512")
    vt = sb("vectors_T", [P, V_ROWS])
    modT = sb("modulation_T", [P, 48])
    gain1 = sb("gain_h1", [P, KD])
    gain2 = sb("gain_h2", [P, KD])
    taps = sb("conv_taps_T", [P, CG, TAPS])
    stat = sb("row_stats", [P, 64])
    d_stat = sb("component_stats", [P, 32])
    top8 = sb("top8", [P, 8])
    wi_s = sb("index_weights", [P, TT, HEADS])
    lam = sb("lambda_parts", [P, 4, 64])
    u_at = region(24576)
    xs_u = sb("scaled_rows", [P, TT, D], at=u_at)
    f_u = sb("feature_rows", [P, KD, SEQ], at=u_at + 8192)
    ada_raw = sb("ada_raw", [P, 2, BLK], at=u_at)
    vec_rows = sb("vector_rows", [P, P], at=u_at + 16384)
    tap_rows = sb("tap_rows", [TAPS, W], at=u_at + 16384 + 512)
    qT = sb("qT", [P, CG, SEQ], at=u_at)
    kT = sb("kT", [P, CG, SEQ], at=u_at + 4096)
    qiT = sb("qiT", [P, CG, SEQ], at=u_at + 8192)
    kiT = sb("kiT", [P, SEQ], at=u_at + 12288)
    ki2 = sb("ki_twice", [P, TT, 2, DH], at=u_at + 13312)
    conv_in = sb("conv_in", [P, CG, PAD + SEQ], at=u_at + 14336)
    conv_out = sb("conv_out", [P, CG, SEQ], at=u_at + 14336 + 4576)
    conv_sq = sb("conv_sq", [P, CG, SEQ], at=u_at + 8192)
    qaT = sb("qaT", [P, CG, SEQ], at=u_at)
    kaT = sb("kaT", [P, CG, SEQ], at=u_at + 4096)
    qbT = sb("qbT", [P, CG, SEQ], at=u_at + 8192)
    kbT = sb("kbT", [P, CG, SEQ], at=u_at + 12288)
    rel_rows = sb("rel_bias_rows", [P, HEADS, SEQ], at=u_at + 16384)
    qxT = sb("qxT", [P, KD, SEQ], at=u_at)
    qx_rows = sb("qx_rows", [P, TT, D], at=u_at + 8192)
    w_at = region(13 * 1024)
    ada_acc = sb("ada_acc", [P, 4, W], at=w_at)
    score = sb("score", [P, TT, SEQ], at=w_at)
    s_work = sb("masked_scores", [P, 2, 2, SEQ], at=w_at + 2048)
    p_work = sb("probabilities", [P, 2, 2, SEQ], at=w_at + 6144)
    pT = sb("probabilities_T", [P, 2, TT, P], at=w_at + 10240)
    bias_t = sb("bias_tile", [P, SEQ], at=w_at + 12288)
    relu_t = sb("relu_tile", [P, 2, SEQ], at=w_at + 6144)
    ff_act = sb("silu_rows", [P, TT, GW], at=w_at)
    ff_hid = sb("hidden_rows", [P, TT, GW], at=w_at + 2048)
    tmp_rows = sb("tmp_rows", [P, TT, W], at=w_at + 4096)
    assert cursor[0] <= 229344, cursor[0]
    y_rows = z[:, :, 0:W]
    y2_rows = z[:, :, W:2 * W]
    merged = z[:, :, 0:D]

    bank = [nc.alloc_psum_tensor(f"bank{i}", [P, W], F32) for i in range(8)]

    def S(name):
        return nc.alloc_semaphore(name)

    raw_landed = [S(f"raw_landed{i}") for i in range(RAW)]
    second_landed = [S(f"second_half_landed{i}") for i in range(RAW)]
    hi_ready, lo_ready, piece_used = S("hi_ready"), S("lo_ready"), S("piece_used")
    acc_free = [S("acc0_free"), S("acc1_free")]
    small_landed = S("small_landed")
    late_landed = S("late_landed")
    final_landed = S("final_landed")
    ada_landed = [S("ada_landed0"), S("ada_landed1")]
    ada_step = S("ada_step")
    nt = {k: S("norm_" + k) for k in ("sumsq", "mean", "rstd", "rows0", "rows1", "turned", "feat_act",
                                      "feat_dve", "hi", "lo")}
    out_done = S("out_done")

    class Named:

        def __init__(self):
            self.made = {}

        def __getitem__(self, name):
            if name not in self.made:
                self.made[name] = S(name)
            return self.made[name]

    sem = Named()
    FAMILIES = [("attention", ("a1_", "b_", "d_", "x_"),
                 {n: (16, 16, 8, 8) for n in ("scores", "max", "negmax", "turned", "pT", "pv")}
                 | {"exp": (16, 16, 16, 8), "bias": (16, 8, 0, 0), "recip": (1, 1, 16, 1)}),
                ("projection", ("m1_", "m2_", "m3_"),
                 {n: (4, 4, 4) for n in ("merged", "merged_turned", "hi", "lo")}),
                ("feed_forward", ("f1_", "f2_"),
                 {n: (2 * NSLAB_FF,) * 2 for n in ("silu", "hidden")}
                 | {n: (NSLAB_FF,) * 2 for n in ("hidden_turned", "hidden_hi", "hidden_lo")})]

    D_BANKS = ((4, 5), (7, 0))

    def family(tag):
        return next(f for f in FAMILIES if tag in f[1])

    def event(tag, name):
        kind, _, counts = family(tag)
        return sem[kind + "_" + name] if name in counts else sem[tag + name]

    def after(tag, name, value):
        _, tags, counts = family(tag)
        base = sum(counts[name][:tags.index(tag)]) if name in counts else 0
        return event(tag, name), base + value

    def slab_src(wt, k0, c0):
        return wt.rearrange("(k p) n -> p k n", p=P)[:, k0:k0 + 4, c0:c0 + W] if isinstance(c0, int) else \
            wt.rearrange("(k p) n -> p k n", p=P)[:, k0:k0 + 4, bass.ds(c0, W)]

    def pair_src(wt, k0, j):
        v = wt.rearrange("(k p) (h n) -> p k h n", p=P, h=2)
        return [v[:, k0:k0 + 4, h, bass.ds(j * GW, GW)] for h in range(2)]

    w2 = {n: a[n].rearrange("o k n -> (o k) n") for n in (
        "w_in", "w_attn_proj", "w_conv_proj", "w_out", "w_ffn_in", "w_ffn_out", "w_ada",
        "w_in_2", "w_up_a_2", "w_up_b_2", "w_out_2", "w_cq_2", "w_ckv_2", "w_co_2", "w_gate_up_2", "w_down_2")}

    STEPS = [(h, t) for h in range(HEADS) for t in range(TT)]

    block = nc.Block()
    ctx = ExitStack()
    ctx.enter_context(block)

    @block.sync
    def _(sp):
        sp.dma_start(mem_rows[:], a["mem_2"].rearrange("o (t p) d -> p (o t) d", p=P)).then_inc(sem["mem_landed"], 16)
        sp.dma_start(const[:], const_dram[:]).then_inc(sem["const_landed"], 16)
        rows = [("c", V_C, 8), ("norm_mix_g", V_MIX, 8), ("norm_ffn_g", V_FFN, 8), ("norm_mix_g_2", V_MIX2, 8),
                ("norm_cross_g_2", V_CROSS, 8), ("norm_mem_g_2", V_MEM, 8), ("norm_ffn_g_2", V_FFN2, 8),
                ("conv_ln_g", V_CLG, 4), ("conv_ln_b", V_CLB, 4), ("b_dw", V_BDW, 4), ("subln_g_2", V_SUB, 1),
                ("b_ada", V_ADA, 48)]
        for name, r, n in rows:
            sp.dma_start(vec_rows[r:r + n, :], a[name].rearrange("o (k p) -> (o k) p", p=P)).then_inc(small_landed, 16)
        sp.dma_start(tap_rows[:], a["w_dw"].rearrange("o t i c -> (o t i) c")).then_inc(small_landed, 16)

        def load(b, src, wide=None, i=0, step=0):
            if b >= RAW:
                sp.wait_ge(lo_ready, last_piece_of(b - RAW) + 1 + i * step)
            dst = raw[:, b % RAW, :]
            if wide == "small":
                dst = dst[:, 0:KD * SMALL].rearrange("p (k n) -> p k n", k=KD)
            elif wide == "pair":
                dst = dst.rearrange("p (k h n) -> p k h n", k=4, h=2)
                sp.dma_start(dst[:, :, 1, :], src[1]).then_inc(second_landed[b % RAW], 16)
                dst, src = dst[:, :, 0, :], src[0]
            elif wide == "long":
                dst = dst.rearrange("p (k n) -> p k n", k=2)
                if pair_blocks(b):
                    sp.dma_start(dst[:, 1, :], src[:, 1, :]).then_inc(second_landed[b % RAW], 16)
                    dst, src = dst[:, 0, :], src[:, 0, :]
            else:
                dst = dst.rearrange("p (k n) -> p k n", k=4)
            sp.dma_start(dst, src).then_inc(raw_landed[b % RAW], 16)

        for s in range(4):
            for k in range(2):
                load(2 * s + k, slab_src(w2["w_ckv_2"], 4 * k, s * W))
            if s == 0:
                sp.dma_start(x[:], a["x"].rearrange("o (t p) d -> p (o t) d", p=P)).then_inc(sem["x_landed"], 16)
        load(8, w2["w_in"].rearrange("(k p) n -> p k n", p=P)[:, :, C_KI:C_U], "small")
        with sp.Fori(0, 2) as i:
            for j in range(4):
                load(9 + j, slab_src(w2["w_in"], 4 * (j % 2), i * (2 * W) + (j // 2) * W), None, i, 8)
        with sp.Fori(0, 3) as i:
            for j in range(4):
                load(17 + j, slab_src(w2["w_in"], 4 * (j % 2), i * (2 * W) + (C_U + (j // 2) * W)), None, i, 8)
        sp.dma_start(final_g[:], a["norm_final_g"].partition_broadcast(P)).then_inc(final_landed, 16)
        for n, name in enumerate(("lam_q1_2", "lam_k1_2", "lam_q2_2", "lam_k2_2")):
            sp.dma_start(lam[:, n, :], a[name].rearrange("o d -> (o d)").partition_broadcast(P)).then_inc(late_landed, 16)
        b = 29
        for c in range(2):
            load(b + c, slab_src(w2["w_attn_proj"], 0, c * W))
        for c in range(2):
            load(b + 2 + c, slab_src(w2["w_conv_proj"], 0, c * W))
        b = 33
        for j in range(4):
            load(b + j, slab_src(w2["w_out"], 4 * (j % 2), (j // 2) * W))

        def load_ff(b, win, wout):
            for j in range(2):
                load(b + j, pair_src(win, 4 * j, 0), "pair")
            with sp.Fori(0, 5) as i:
                for j in range(4):
                    load(b + 2 + j, pair_src(win, 4 * (j % 2), i * 2 + (1 + j // 2)), "pair", i, 8)
            b += 22
            v = wout.rearrange("(k p) n -> p k n", p=P)
            for j in range(3):
                load(b + j, v[:, 2 * j:2 * j + 2, :], "long")
            with sp.Fori(0, 2) as i:
                for j in range(4):
                    load(b + 3 + j, v[:, bass.ds(i * 8 + (6 + 2 * j), 2), :], "long", i, 8)

        load_ff(37, w2["w_ffn_in"], w2["w_ffn_out"])
        with sp.Fori(0, 5) as i:
            for j in range(4):
                load(70 + j, slab_src(w2["w_in_2"], 4 * (j % 2), i * (2 * W) + (j // 2) * W), None, i, 8)
        rb = a["rel_bias_2"].rearrange("o h r -> (o h) r")
        sp.wait_ge(sem["conv_lo"], 1)
        src = bass.AP(tensor=rb.tensor, offset=rb.offset + 1 + P, ap=[[1, P], [2 * SEQ + 1, HEADS], [1, SEQ]])
        sp.dma_start(rel_rows[:], src).then_inc(sem["rel_landed"], 16)
        for n, name in ((90, "w_up_a_2"), (92, "w_up_b_2")):
            for c in range(2):
                load(n + c, slab_src(w2[name], 0, c * W))
        for n, name in ((94, "w_out_2"), (98, "w_cq_2"), (102, "w_co_2")):
            for j in range(4):
                load(n + j, slab_src(w2[name], 4 * (j % 2), (j // 2) * W))
            if n == 94:
                sp.wait_ge(sem["final1_done"], TT)
                sp.dma_start(final_g[:], a["norm_final_g_2"].partition_broadcast(P)).then_inc(final_landed, 16)
        load_ff(106, w2["w_gate_up_2"], w2["w_down_2"])
        for t in range(TT):
            sp.wait_ge(sem["result"], t + 1)
            sp.dma_start(out.rearrange("o (t p) d -> p (o t) d", p=P)[:, t, :], x[:, t, :]).then_inc(out_done, 16)
        sp.wait_ge(out_done, 16 * TT)

    @block.gpsimd
    def _(pool):
        for m, g in ((2, g_mix), (5, g_ffn)):
            pool.dma_start(g[:], a["b_ada"].rearrange("o n -> (o n)")[m * D:(m + 1) * D].partition_broadcast(P))\
                .then_inc(sem["gate_bias_landed"], 16)

        def ada_block(n, s, k, i=0, step=0, wait=True):
            if wait:
                pool.wait_ge(ada_step, 4 * (n - 1) + i * (4 * step))
            pool.dma_start(ada_raw[:, n % 2, :].rearrange("p (k n) -> p k n", k=4),
                           slab_src(w2["w_ada"], 4 * k, s)).then_inc(ada_landed[n % 2], 16)

        def rstd(n):
            pool.wait_ge(nt["mean"], n + 1)
            pool.tensor_tensor(stat[:, 4:6], stat[:, 2:4], C("half", 0, 2), ALU.pow).then_inc(nt["rstd"], 1)

        for k in range(2):
            ada_block(k, 0, k, wait=False)
        pool.wait_ge(sem["const_landed"], 16)
        rstd(N_MEM)
        for n in range(2, 8):
            if n == 4:
                rstd(N_H1)
            ada_block(n, (n // 2) * W, n % 2)
        with pool.Fori(0, 8) as i:
            for k in range(2):
                ada_block(8 + k, i * W + 4 * W, k, i, 2)
        pool.wait_ge(sem["ln_var"], 1)
        pool.tensor_tensor(conv_sq[:, 1, :], conv_sq[:, 0, :], C("half"), ALU.pow).then_inc(sem["ln_rstd"], 1)
        rstd(N_H2)
        rstd(N_FINAL1)
        rstd(N_M2)
        pool.wait_ge(sem["sub_mean"], 1)
        pool.tensor_tensor(stat[:, 24:32], stat[:, 16:24], C("half", 0, 8), ALU.pow).then_inc(sem["sub_rstd"], 1)
        rstd(N_CR)
        rstd(N_F2)
        rstd(N_FINAL2)

    @block.tensor
    def _(pe):
        def mm3(ps, kt, t, hi, lo, wh, wl, start, stop):
            ts = slice(t * P, (t + 1) * P)
            pe.matmul(ps, hi[:, kt, ts], wh, start=start, stop=False)
            pe.matmul(ps, hi[:, kt, ts], wl, start=False, stop=False)
            return pe.matmul(ps, lo[:, kt, ts], wh, start=False, stop=stop)

        def piece(p, u, j, n, i=0, kbase=0, norm=None, ready=None, hidden=None):
            pe.wait_ge(lo_ready, p + 1 + i * 8)
            if norm is not None:
                pe.wait_ge(nt["lo"], 4 * F_OF[norm] + j + 1)
            if ready is not None:
                pe.wait_ge(*ready)
            if j == 0 and u >= 2 and hidden is None:
                for t in range(TT):
                    pe.wait_ge(acc_free[t], u - 1 + i * 2)
            elif j == 0 and hidden is not None:
                pe.wait_ge(hidden[0], hidden[1] + i * 4)
            wh = w_hi[:, p % RING, :].rearrange("p (k n) -> p k n", k=2)
            wl = w_lo[:, p % RING, :].rearrange("p (k n) -> p k n", k=2)
            for kk in range(2):
                kt = 2 * j + kk
                for t in range(TT):
                    last = mm3(bank[2 * (u % 2) + t][:], kbase + kt, t, a_hi, a_lo, wh[:, kk, :], wl[:, kk, :],
                               kt == 0, kt == 2 * n - 1)
            last.then_inc(piece_used, 1)

        def slab(p, u, i=0, norm=None):
            for j in range(4):
                piece(p + j, u, j, 4, i, 0, norm)

        def turn(n, src):
            for g in range(4):
                if g == 0:
                    pe.wait_ge(nt["rows0"], F_OF[n] + 1)
                    pe.wait_ge(nt["rows1"], F_OF[n] + 1)
                for kk in range(2):
                    kt = 2 * g + kk
                    for t in range(TT):
                        last = pe.transpose(bank[4 + g][:, kk * SEQ + t * P:kk * SEQ + (t + 1) * P],
                                            src[:, t, kt * P:(kt + 1) * P], ident)
                last.then_inc(nt["turned"], 1)

        def turn4(b0, src_cols, src, done, n=CG):
            for g in range((n + 1) // 2):
                for kk in range(min(2, n - 2 * g)):
                    c = src_cols + (2 * g + kk) * P
                    for t in range(TT):
                        last = pe.transpose(bank[b0 + g][:, kk * SEQ + t * P:kk * SEQ + (t + 1) * P],
                                            src[:, t, c:c + P], ident)
                last.then_inc(done, 1)

        pe.wait_ge(sem["const_landed"], 16)
        pe.wait_ge(small_landed, 16 * 13)
        pe.transpose(bank[7][:, 0:V_ROWS], vec_rows[0:V_ROWS, :], ident[0:V_ROWS, 0:V_ROWS])
        for g in range(CG):
            last = pe.transpose(bank[7][:, P + g * TAPS:P + (g + 1) * TAPS], tap_rows[:, g * P:(g + 1) * P],
                                ident[0:TAPS, 0:TAPS])
        last.then_inc(sem["vec_turned"], 1)
        pe.wait_ge(sem["vec_copied"], 2)
        turn(N_MEM, xs_z)
        for s in range(4):
            slab(P_CKV + 4 * s, U_CKV + s, norm=N_MEM if s == 0 else None)
            if s == 2:
                pe.wait_ge(acc_free[0], 2)
                pe.wait_ge(acc_free[1], 2)
                for g in range(4):
                    for kk in range(2):
                        kt = 2 * g + kk
                        for t in range(TT):
                            last = pe.transpose(bank[4 + g][:, kk * SEQ + t * P:kk * SEQ + (t + 1) * P],
                                                k_rows[:, t, kt * P:(kt + 1) * P], ident)
                    last.then_inc(sem["key_turned"], 1)
        pe.wait_ge(ada_step, 8 * 4)
        pe.wait_ge(sem["key_copied"], 4)
        for j in range(16):
            last = pe.matmul(bank[4][:, j:j + 1], ada_acc[:, j // 4, (j % 4) * P:(j % 4 + 1) * P], ones[:, 0:1],
                             start=True, stop=True)
        last.then_inc(sem["ada_reduced"], 1)
        pe.wait_ge(sem["mod_copied"], 1)
        turn(N_H1, xs_z)
        pe.wait_ge(lo_ready, P_SMALL + 1)
        for t in range(TT):
            pe.wait_ge(acc_free[t], U_SMALL - 1)
        pe.wait_ge(nt["lo"], 4 * N_H1 + 4)
        sm_hi = w_hi[:, P_SMALL % RING, 0:KD * SMALL].rearrange("p (k n) -> p k n", k=KD)
        sm_lo = w_lo[:, P_SMALL % RING, 0:KD * SMALL].rearrange("p (k n) -> p k n", k=KD)
        for t in range(TT):
            for kt in range(KD):
                last = mm3(bank[2 * (U_SMALL % 2) + t][:, 0:SMALL], kt, t, a_hi, a_lo, sm_hi[:, kt, :],
                           sm_lo[:, kt, :], kt == 0, kt == KD - 1)
        last.then_inc(piece_used, 1)
        with pe.Fori(0, 2) as i:
            for s in range(2):
                slab(P_IN1 + 4 * s, U_IN1 + s, i)
        def reduce_gate(step, n):
            pe.wait_ge(ada_step, step)
            pe.wait_ge(sem["mod_copied"], n)
            for c in range(2):
                pe.matmul(bank[5 + c][:], ones, ada_acc[:, 2 * (n == 2) + c, :], start=True, stop=True)
            for j in range(8):
                s = 2 * (n == 1) + j // 4
                last = pe.matmul(bank[4][:, j:j + 1], ada_acc[:, s, (j % 4) * P:(j % 4 + 1) * P],
                                 ones[:, 0:1], start=True, stop=True)
            last.then_inc(sem["ada_reduced"], 1)

        reduce_gate(8 * 8, 1)
        with pe.Fori(0, 3) as i:
            for s in range(2):
                slab(P_IN1 + 16 + 4 * s, U_IN1 + 4 + s, i)
        reduce_gate(8 * 12, 2)
        pe.wait_ge(sem["mod_copied"], 3)
        pe.wait_ge(acc_free[0], U_IN1 + 10)
        pe.wait_ge(acc_free[1], U_IN1 + 10)
        pe.wait_ge(sem["ki_copied"], 1)
        turn4(4, C_QI, z, sem["t1"])
        for t in range(TT):
            last = pe.transpose(bank[6][:, t * P:(t + 1) * P], ki2[:, t, :, :].rearrange("p a d -> p (a d)"), ident)
        last.then_inc(sem["t1"], 1)
        turn4(0, C_Q, z, sem["t1"])
        turn4(2, C_K, z, sem["t1"])
        pe.wait_ge(sem["t1_copied_act"], 4)
        pe.wait_ge(sem["t1_copied_dve"], 3)
        for n, (t, h) in enumerate([(t, h) for t in range(TT) for h in range(HEADS)]):
            keys = P * (t + 1)
            if n >= 2:
                pe.wait_ge(sem["relu_done"], n - 1)
            half = slice(64 * (h % 2), 64 * (h % 2) + 64)
            pe.matmul(bank[4 + n % 2][:, 0:keys], qiT[half, h // 2, t * P:(t + 1) * P], kiT[half, 0:keys],
                      start=True, stop=True).then_inc(sem["logits"], 1)
        pe.wait_ge(sem["glu"], TT)
        turn4(6, C_U, z, sem["conv_turned"])

        def attention(tag, q, k, v_cols, pv_banks, base):
            def scores(n):
                h, t = STEPS[n]
                keys = P * (t + 1)
                half = slice(64 * (h % 2), 64 * (h % 2) + 64)
                if n >= 2:
                    pe.wait_ge(*after(tag, "max", n - 1))
                pe.matmul(bank[4 + n % 2][:, 0:keys], q[half, h // 2, t * P:(t + 1) * P], k[half, h // 2, 0:keys],
                          start=True, stop=True).then_inc(event(tag, "scores"), 1)

            def turn_p(n):
                h, t = STEPS[n]
                pe.wait_ge(*after(tag, "exp", n + 1))
                if n >= 1:
                    pe.wait_ge(*after(tag, "pT", n))
                for kt in range(t + 1):
                    last = pe.transpose(bank[6][:, kt * P:(kt + 1) * P], p_work[:, n % 2, 0, kt * P:(kt + 1) * P], ident)
                last.then_inc(event(tag, "turned"), 1)

            def values(n):
                h, t = STEPS[n]
                pe.wait_ge(*after(tag, "pT", n + 1))
                for kt in range(t + 1):
                    last = pe.matmul(bank[pv_banks + t][:, h * DH:(h + 1) * DH], pT[:, n % 2, kt, :],
                                     z[:, kt, v_cols + h * DH:v_cols + (h + 1) * DH],
                                     start=(kt == 0), stop=(kt == t))
                last.then_inc(event(tag, "pv"), 1)

            scores(0)
            for n in range(len(STEPS)):
                if n + 1 < len(STEPS):
                    scores(n + 1)
                turn_p(n)
                if n >= 1:
                    values(n - 1)
            values(len(STEPS) - 1)

        pe.wait_ge(sem["relu_done"], 16)
        attention("a1_", qT, kT, C_V, 0, 0)
        pe.wait_ge(sem["conv_done"], 4 * TAPS)
        pe.wait_ge(*after("a1_", "max", 16))
        for g in range(CG):
            last = pe.matmul(bank[4][:, 0:SEQ], mean512, conv_out[:, g, :], start=(g == 0), stop=(g == CG - 1))
        last.then_inc(sem["ln_mean"], 1)
        pe.wait_ge(sem["ln_square"], 1)
        for g in range(CG):
            last = pe.matmul(bank[5][:, 0:SEQ], mean512, conv_sq[:, g, :], start=(g == 0), stop=(g == CG - 1))
        last.then_inc(sem["ln_sumsq"], 1)

        pe.wait_ge(sem["y1"], TT)
        turn4(6, 0, z, sem["y1_turned"])
        def two_halves(p, u, ready, kbase):
            for c in range(2):
                for j in range(2):
                    piece(p + 2 * c + j, u + c, j, 2, 0, kbase, None, ready)

        two_halves(P_PA, U_PA, (sem["y1_lo"], 2), 0)
        two_halves(P_PC, U_PC, (sem["conv_lo"], 1), 4)

        def turn_merged(tag):
            for g in range(4):
                if g % 2 == 0:
                    pe.wait_ge(*after(tag, "merged", TT * (g // 2 + 1)))
                for kk in range(2):
                    kt = 2 * g + kk
                    for t in range(TT):
                        last = pe.transpose(bank[4 + g][:, kk * SEQ + t * P:kk * SEQ + (t + 1) * P],
                                            z[:, t, kt * P:(kt + 1) * P], ident)
                last.then_inc(event(tag, "merged_turned"), 1)

        def project(p, u, tag):
            for s in range(2):
                for j in range(4):
                    piece(p + 4 * s + j, u + s, j, 4, 0, 0, None, after(tag, "lo", j + 1) if s == 0 else None)

        turn_merged("m1_")
        project(P_OUT1, U_OUT1, "m1_")
        turn(N_H2, xs_u)

        def feed_forward(p, u, norm, tag):
            def turn_hidden(s, wait, i=0):
                pe.wait_ge(*after(tag, "hidden", wait + i * 4))
                for kk in range(2):
                    for t in range(TT):
                        last = pe.transpose(bank[4 + s % 2][:, kk * SEQ + t * P:kk * SEQ + (t + 1) * P],
                                            ff_hid[:, t, kk * P:(kk + 1) * P], ident)
                last.then_inc(event(tag, "hidden_turned"), 1)

            slab(p, u, 0, norm)
            for t in range(TT):
                pe.wait_ge(acc_free[t], u)
            with pe.Fori(0, 5) as i:
                for s in (1, 2):
                    for j in range(4):
                        piece(p + 4 * s + j, u + s, j, 4, i, hidden=after(tag, "hidden", TT * (s - 1)))
                        if j == 1:
                            turn_hidden(s - 1, TT * s, i)
            p += 4 * NSLAB_FF
            pe.wait_ge(*after(tag, "hidden", TT * NSLAB_FF))
            for kt in range(KF):
                if kt == 2:
                    turn_hidden(NSLAB_FF - 1, TT * NSLAB_FF)
                pe.wait_ge(lo_ready, p + kt + 1)
                pe.wait_ge(*after(tag, "hidden_lo", kt // 2 + 1))
                wh, wl = w_hi[:, (p + kt) % RING, :], w_lo[:, (p + kt) % RING, :]
                for t in range(TT):
                    ts = slice(t * P, (t + 1) * P)
                    for n, (lhs, w) in enumerate(((f_hi, wh), (f_hi, wl), (f_lo, wh))):
                        for c in range(2):
                            last = pe.matmul(bank[2 * t + c][:], lhs[:, kt, ts], w[:, c * W:(c + 1) * W],
                                             start=(kt == 0 and n == 0), stop=(kt == KF - 1 and n == 2))
                last.then_inc(piece_used, 1)

        feed_forward(P_FI1, U_FI1, N_H2, "f1_")
        turn(N_M2, xs_u)
        pe.wait_ge(nt["lo"], 4 * F_OF[N_M2] + 4)
        with pe.Fori(0, 5) as i:
            for s in range(2):
                slab(P_IN2 + 4 * s, U_IN2 + s, i)

        pe.wait_ge(acc_free[0], U_IN2 + 10)
        pe.wait_ge(acc_free[1], U_IN2 + 10)
        turn4(4, E_QB, z, sem["t2"])
        turn4(6, E_KB, z, sem["t2"])
        pe.wait_ge(sem["rope_sum"], TT)
        turn4(0, E_QA, z, sem["t2"])
        turn4(2, E_KA, z, sem["t2"])
        pe.wait_ge(sem["t2_copied_act"], 4)
        pe.wait_ge(sem["t2_copied_dve"], 4)
        attention("b_", qbT, kbT, E_VB, 0, 0)

        DS = [(h, t) for h in range(4) for t in range(TT)]

        def d_scores(n):
            h, t = DS[n]
            keys = P * (t + 1)
            if n >= 2:
                pe.wait_ge(*after("d_", "max", n - 1))
            if n == 1:
                pe.wait_ge(sem["yb"], TT)
            for c in range(2):
                half = slice(64 * c, 64 * c + 64)
                last = pe.matmul(bank[D_BANKS[n % 2][c]][:, 0:keys], qaT[half, h, t * P:(t + 1) * P],
                                 kaT[half, h, 0:keys], start=True, stop=True)
            last.then_inc(event("d_", "scores"), 1)

        def d_turn(n):
            h, t = DS[n]
            pe.wait_ge(*after("d_", "mix", n + 1))
            if n >= 1:
                pe.wait_ge(*after("d_", "pT", n))
            for kt in range(t + 1):
                last = pe.transpose(bank[6][:, kt * P:(kt + 1) * P], p_work[:, n % 2, 0, kt * P:(kt + 1) * P], ident)
            last.then_inc(event("d_", "turned"), 1)

        def d_values(n):
            h, t = DS[n]
            pe.wait_ge(*after("d_", "pT", n + 1))
            for kt in range(t + 1):
                last = pe.matmul(bank[2 + t][:, h * P:(h + 1) * P], pT[:, n % 2, kt, :],
                                 z[:, kt, E_VA + h * P:E_VA + (h + 1) * P], start=(kt == 0), stop=(kt == t))
            last.then_inc(event("d_", "pv"), 1)

        pe.wait_ge(*after("b_", "max", 16))
        pe.wait_ge(*after("b_", "pT", 16))
        d_scores(0)
        for n in range(len(DS)):
            if n + 1 < len(DS):
                d_scores(n + 1)
            d_turn(n)
            if n >= 1:
                d_values(n - 1)
        d_values(len(DS) - 1)
        pe.wait_ge(sem["ya"], TT)
        turn4(4, 0, z, sem["y2_turned"])
        pe.wait_ge(sem["yb"], TT)
        pe.wait_ge(*after("d_", "pT", 8))
        turn4(6, W, z, sem["y2_turned"])
        two_halves(P_UA, U_UA, (sem["y2_lo"], 2), 0)
        two_halves(P_UB, U_UB, (sem["y2_lo"], 4), 4)
        turn_merged("m2_")
        project(P_OUT2, U_OUT2, "m2_")

        turn(N_CR, xs_u)
        for s in range(2):
            slab(P_CQ + 4 * s, U_CQ + s, 0, (N_CR) if s == 0 else None)
        pe.wait_ge(acc_free[0], U_CQ + 2)
        pe.wait_ge(acc_free[1], U_CQ + 2)
        for g in range(4):
            for kk in range(2):
                kt = 2 * g + kk
                for t in range(TT):
                    last = pe.transpose(bank[4 + g][:, kk * SEQ + t * P:kk * SEQ + (t + 1) * P],
                                        qx_rows[:, t, kt * P:(kt + 1) * P], ident)
            last.then_inc(sem["qx_turned"], 1)

        def x_scores(n):
            h, t = DS[n]
            if n >= 2:
                pe.wait_ge(*after("x_", "exp", n - 1))
            for kk in range(2):
                last = pe.matmul(bank[4 + n % 2][:, 0:SEQ], qxT[:, 2 * h + kk, t * P:(t + 1) * P],
                                 mem_kT[:, 2 * h + kk, :], start=(kk == 0), stop=(kk == 1))
            last.then_inc(event("x_", "scores"), 1)

        def x_turn(n):
            pe.wait_ge(*after("x_", "exp", n + 1))
            if n >= 1:
                pe.wait_ge(*after("x_", "pT", n))
            for kt in range(TT):
                last = pe.transpose(bank[6][:, kt * P:(kt + 1) * P], p_work[:, n % 2, 0, kt * P:(kt + 1) * P], ident)
            last.then_inc(event("x_", "turned"), 1)

        def x_values(n):
            h, t = DS[n]
            pe.wait_ge(*after("x_", "pT", n + 1))
            for kt in range(TT):
                last = pe.matmul(bank[2 * (h // 2) + t][:, (h % 2) * SEQ:(h % 2 + 1) * SEQ], pT[:, n % 2, kt, :],
                                 mem_v[:, kt, h * SEQ:(h + 1) * SEQ], start=(kt == 0), stop=(kt == TT - 1))
            last.then_inc(event("x_", "pv"), 1)

        pe.wait_ge(sem["qx_copied_act"], 2)
        pe.wait_ge(sem["qx_copied_dve"], 2)
        x_scores(0)
        for n in range(len(DS)):
            if n + 1 < len(DS):
                x_scores(n + 1)
            x_turn(n)
            if n >= 1:
                x_values(n - 1)
        x_values(len(DS) - 1)
        pe.wait_ge(*after("x_", "pT", 8))
        turn_merged("m3_")
        project(P_CO, U_CO, "m3_")
        turn(N_F2, xs_u)
        feed_forward(P_FI2, U_FI2, N_F2, "f2_")

    @block.scalar
    def _(act):
        def conv(p, n=1, i=0):
            for q in range(p, p + n):
                b, half = block_of(q)
                act.wait_ge(raw_landed[b % RAW], 16 * (b // RAW + 1) + i * 16)
                if pair_blocks(b):
                    act.wait_ge(second_landed[b % RAW], 16 * pair_blocks(b) + i * 16)
                if q >= RING:
                    act.wait_ge(piece_used, q - RING + 1 + i * 8)
                m = KD * SMALL if q == P_SMALL else PIECE
                act.activation(w_hi[:, q % RING, 0:m], raw[:, b % RAW, half * PIECE:half * PIECE + m], ACT.Copy)\
                    .then_inc(hi_ready, 1)

        def two(b):
            return bank[b][:].rearrange("p (k n) -> p k n", k=2)

        def updated(count):
            return lambda t: (acc_free[t], count)

        def sumsq(n, src, junk, done=None):
            for t in range(TT):
                if done is not None:
                    act.wait_ge(*done(t))
                act.activation(junk[:, t, :], src[:, t, :], ACT.Square, accum_out=stat[:, t:t + 1])\
                    .then_inc(nt["sumsq"], 1)

        def rows1(n, src, dst):
            act.wait_ge(nt["rstd"], n + 1)
            act.wait_ge(nt["sumsq"], TT * (n + 1))
            act.activation(dst[:, 1, :], src[:, 1, :], ACT.Copy, scale=stat[:, 5:6]).then_inc(nt["rows1"], 1)

        def features(n, f, gain, shift, between=None):
            fi = F_OF[n]
            for g in (0, 2):
                act.wait_ge(nt["turned"], 4 * fi + g + 1)
                for kk in range(2):
                    kt = 2 * g + kk
                    last = act.activation(f[:, kt, :], bank[4 + g][:, kk * SEQ:(kk + 1) * SEQ], ACT.Identity,
                                          scale=gain[:, kt:kt + 1],
                                          bias=0.0 if shift is None else shift[:, kt:kt + 1])
                last.then_inc(nt["feat_act"], 1)
            for g in range(4):
                act.wait_ge(nt["feat_dve" if g % 2 else "feat_act"], 2 * fi + g // 2 + 1)
                act.activation(a_hi[:, 2 * g:2 * g + 2, :], f[:, 2 * g:2 * g + 2, :], ACT.Copy).then_inc(nt["hi"], 1)
                if between is not None:
                    conv(between + g)

        def copy_pair(done, n, dst, b, copied):
            act.wait_ge(done, n)
            act.activation(dst, two(b), ACT.Copy).then_inc(copied, 1)

        act.wait_ge(sem["mem_landed"], 16)
        sumsq(N_MEM, mem_rows, xs_z)
        rows1(N_MEM, mem_rows, xs_z)
        act.wait_ge(sem["vec_copied"], 1)
        act.activation(stat[:, 8:16], vt[:, V_C:V_C + 8], ACT.Silu).then_inc(sem["c_act"], 1)
        features(N_MEM, f_z, vt[:, V_MEM:V_MEM + 8], None, P_CKV)
        for s in range(4):
            if s < 3:
                conv(P_CKV + 4 * s + 4, 4)
            else:
                conv(P_SMALL)
            act.wait_ge(piece_used, P_CKV + 4 * s + 4)
            dst = k_rows if s < 2 else mem_v
            act.activation(dst[:, 0, (s % 2) * W:(s % 2 + 1) * W], bank[2 * (s % 2)][:], ACT.Copy)\
                .then_inc(acc_free[0], 1)
            if s == 2:
                for g in (0, 2):
                    copy_pair(sem["key_turned"], g + 1, mem_kT[:, 2 * g:2 * g + 2, :], 4 + g, sem["key_copied"])
            if s == 0:
                act.wait_ge(sem["x_landed"], 16)
                sumsq(N_H1, x, xs_z)
                rows1(N_H1, x, xs_z)
        act.wait_ge(sem["gains"], 1)
        features(N_H1, f_z, gain1, modT[:, 0:8])
        conv(P_IN1, 4)
        act.wait_ge(piece_used, P_SMALL + 1)
        act.activation(z[:, 0, C_KI:C_U], bank[2 * (U_SMALL % 2)][:, 0:SMALL], ACT.Copy).then_inc(acc_free[0], 1)

        def project_slabs(p, u, c0, n):
            with act.Fori(0, n // 2) as i:
                for s in range(2):
                    conv(p + 4 * s + 4, 4, i)
                    act.wait_ge(piece_used, p + 4 * s + 4 + i * 8)
                    act.activation(z[:, 0, bass.ds(i * (2 * W) + (c0 + s * W), W)], bank[2 * ((u + s) % 2)][:],
                                   ACT.Copy).then_inc(acc_free[0], 1)

        project_slabs(P_IN1, U_IN1, 0, 4)
        project_slabs(P_IN1 + 16, U_IN1 + 4, C_U, 6)

        copy_pair(sem["t1"], 1, qiT[:, 0:2, :], 4, sem["t1_copied_act"])
        act.wait_ge(sem["t1"], 3)
        act.activation(kiT[:], bank[6][:, 0:SEQ], ACT.Copy).then_inc(sem["t1_copied_act"], 1)
        copy_pair(sem["t1"], 4, qT[:, 0:2, :], 0, sem["t1_copied_act"])
        copy_pair(sem["t1"], 6, kT[:, 0:2, :], 2, sem["t1_copied_act"])
        for n in range(TT * HEADS):
            keys = P * (n // HEADS + 1)
            act.wait_ge(sem["logits"], n + 1)
            if n >= 2:
                act.wait_ge(sem["score_step"], n - 1)
            act.activation(relu_t[:, n % 2, 0:keys], bank[4 + n % 2][:, 0:keys], ACT.Relu, scale=DH ** -0.5)\
                .then_inc(sem["relu_done"], 1)
        act.wait_ge(acc_free[0], U_IN1 + 10)
        act.wait_ge(acc_free[1], U_IN1 + 10)
        for t in range(TT):
            act.activation(z[:, t, C_U + W:C_U + 2 * W], z[:, t, C_U + W:C_U + 2 * W], ACT.Sigmoid)\
                .then_inc(sem["sig_u"], 1)
        for t in range(TT):
            act.activation(z[:, t, C_GA:C_GA + 2 * D], z[:, t, C_GA:C_GA + 2 * D], ACT.Sigmoid)\
                .then_inc(sem["sig_gates"], 1)
        act.wait_ge(sem["conv_turned"], 1)
        act.wait_ge(sem["pad_zeroed"], 1)
        act.activation(conv_in[:, 0:2, PAD:], two(6), ACT.Copy).then_inc(sem["conv_in_act"], 1)

        def softmax_steps(tag):
            for n, (h, t) in enumerate(STEPS):
                keys = P * (t + 1)
                act.wait_ge(*after(tag, "negmax", n + 1))
                if n >= 2:
                    act.wait_ge(*after(tag, "turned", n - 1))
                act.activation(p_work[:, n % 2, 0, 0:keys], s_work[:, n % 2, 0, 0:keys], ACT.Exp,
                               bias=stat[:, 34 + n % 2:35 + n % 2], accum_out=stat[:, 36 + t * 8 + h:37 + t * 8 + h])\
                    .then_inc(event(tag, "exp"), 1)
                act.wait_ge(*after(tag, "turned", n + 1))
                if n >= 2:
                    act.wait_ge(*after(tag, "pv", n - 1))
                act.activation(pT[:, n % 2, 0:t + 1, :], bank[6][:, 0:keys].rearrange("p (k n) -> p k n", k=t + 1),
                               ACT.Copy).then_inc(event(tag, "pT"), 1)

        softmax_steps("a1_")
        act.wait_ge(sem["ln_scaled"], 1)
        for g in range(CG):
            last = act.activation(conv_in[:, g, 0:SEQ], conv_out[:, g, :], ACT.Silu,
                                  scale=vt[:, V_CLG + g:V_CLG + g + 1], bias=vt[:, V_CLB + g:V_CLB + g + 1])
        last.then_inc(sem["swish"], 1)
        act.wait_ge(sem["swish"], 1)
        act.activation(a_hi[:, 4:8, :], conv_in[:, :, 0:SEQ], ACT.Copy).then_inc(sem["conv_hi"], 1)
        for g in range(2):
            act.wait_ge(sem["y1_turned"], g + 1)
            act.activation(a_hi[:, 2 * g:2 * g + 2, :], two(6 + g), ACT.Copy).then_inc(sem["y1_hi"], 1)
        conv(P_PC, 4)
        conv(P_OUT1, 4)

        def merged_hi(tag):
            for g in range(4):
                act.wait_ge(*after(tag, "merged_turned", g + 1))
                act.activation(a_hi[:, 2 * g:2 * g + 2, :], two(4 + g), ACT.Copy).then_inc(event(tag, "hi"), 1)

        merged_hi("m1_")
        conv(P_OUT1 + 4, 4)
        conv(P_FI1, 4)
        sumsq(N_H2, x, xs_u, updated(U_OUT1 + 2))
        rows1(N_H2, x, xs_u)
        features(N_H2, f_u, gain2, modT[:, 24:32])

        def feed_forward(p, u, tag, following):
            def silu(s, i=0):
                act.wait_ge(piece_used, p + 4 * s + 4 + i * 8)
                for t in range(TT):
                    act.activation(ff_act[:, t, :], bank[2 * ((u + s) % 2) + t][:, 0:GW], ACT.Silu)\
                        .then_inc(event(tag, "silu"), 1)

            def hidden_hi(s, dst, i=0):
                act.wait_ge(*after(tag, "hidden_turned", s + 1 + i * 2))
                act.activation(dst, two(4 + s % 2), ACT.Copy).then_inc(event(tag, "hidden_hi"), 1)

            conv(p + 4, 4)
            with act.Fori(0, 5) as i:
                for s in (1, 2):
                    silu(s - 1, i)
                    conv(p + 4 * s + 4, 2, i)
                    hidden_hi(s - 1, f_hi[:, bass.ds(i * 4 + (2 * s - 2), 2), :], i)
                    conv(p + 4 * s + 6, 2, i)
            last = NSLAB_FF - 1
            silu(last)
            p += 4 * NSLAB_FF
            conv(p + 4, 2)
            hidden_hi(last, f_hi[:, 2 * last:2 * last + 2, :])
            with act.Fori(0, 2) as i:
                conv(p + 6, 8, i)
            conv(p + KF, following)

        feed_forward(P_FI1, U_FI1, "f1_", 4)
        sumsq(N_FINAL1, x, xs_u, updated(U_FI1 + 2))
        sumsq(N_M2, x, xs_u, lambda t: (sem["final1_done"], t + 1))
        rows1(N_M2, x, xs_u)
        features(N_M2, f_u, vt[:, V_MIX2:V_MIX2 + 8], None)
        project_slabs(P_IN2, U_IN2, 0, 10)

        copy_pair(sem["t2"], 1, qbT[:, 0:2, :], 4, sem["t2_copied_act"])
        copy_pair(sem["t2"], 3, kbT[:, 0:2, :], 6, sem["t2_copied_act"])
        act.wait_ge(sem["lam_dots"], 2)
        act.activation(stat[:, 56:58], stat[:, 54:56], ACT.Exp).then_inc(sem["lam_exp"], 1)
        copy_pair(sem["t2"], 5, qaT[:, 0:2, :], 0, sem["t2_copied_act"])
        copy_pair(sem["t2"], 7, kaT[:, 0:2, :], 2, sem["t2_copied_act"])
        softmax_steps("b_")
        for n in range(8):
            keys = P * (n % 2 + 1)
            act.wait_ge(*after("d_", "negmax", n + 1))
            if n >= 2:
                act.wait_ge(*after("d_", "turned", n - 1))
            for c in range(2):
                k = 2 * (n % 2) + c
                act.activation(p_work[:, n % 2, c, 0:keys], s_work[:, n % 2, c, 0:keys], ACT.Exp,
                               bias=d_stat[:, 4 + k:5 + k], accum_out=d_stat[:, 8 + k:9 + k]).then_inc(event("d_", "exp"), 1)
            act.wait_ge(*after("d_", "turned", n + 1))
            if n >= 2:
                act.wait_ge(*after("d_", "pv", n - 1))
            act.activation(pT[:, n % 2, 0:n % 2 + 1, :], bank[6][:, 0:keys].rearrange("p (k n) -> p k n", k=n % 2 + 1),
                           ACT.Copy).then_inc(event("d_", "pT"), 1)
        for t in range(TT):
            act.activation(z[:, t, E_GA:E_GA + 2 * D], z[:, t, E_GA:E_GA + 2 * D], ACT.Sigmoid)\
                .then_inc(sem["sig_gates2"], 1)
        for g in range(2):
            act.wait_ge(sem["ya_feat"], g + 1)
            act.activation(a_hi[:, 2 * g:2 * g + 2, :], f_u[:, 2 * g:2 * g + 2, :], ACT.Copy).then_inc(sem["y2_hi"], 1)
        for g in range(2):
            act.wait_ge(sem["y2_turned"], 3 + g)
            act.activation(a_hi[:, 4 + 2 * g:6 + 2 * g, :], two(6 + g), ACT.Copy).then_inc(sem["y2_hi"], 1)
        conv(P_UB, 4)
        conv(P_OUT2, 4)
        merged_hi("m2_")
        conv(P_OUT2 + 4, 4)
        conv(P_CQ, 4)
        sumsq(N_CR, x, xs_u, updated(U_OUT2 + 2))
        rows1(N_CR, x, xs_u)
        features(N_CR, f_u, vt[:, V_CROSS:V_CROSS + 8], None)
        for s in range(2):
            conv(P_CQ + 4 + 4 * s, 4)
            act.wait_ge(piece_used, P_CQ + 4 * s + 4)
            act.activation(qx_rows[:, 0, s * W:(s + 1) * W], bank[2 * ((U_CQ + s) % 2)][:], ACT.Copy)\
                .then_inc(acc_free[0], 1)
        for g in (0, 2):
            copy_pair(sem["qx_turned"], g + 1, qxT[:, 2 * g:2 * g + 2, :], 4 + g, sem["qx_copied_act"])
        for n in range(8):
            h, t = n // 2, n % 2
            act.wait_ge(*after("x_", "negmax", n + 1))
            if n >= 2:
                act.wait_ge(*after("x_", "turned", n - 1))
            act.activation(p_work[:, n % 2, 0, :], bank[4 + n % 2][:, 0:SEQ], ACT.Exp, scale=1.0 / 16,
                           bias=stat[:, 34 + n % 2:35 + n % 2], accum_out=stat[:, 36 + t * 4 + h:37 + t * 4 + h])\
                .then_inc(event("x_", "exp"), 1)
            act.wait_ge(*after("x_", "turned", n + 1))
            if n >= 2:
                act.wait_ge(*after("x_", "pv", n - 1))
            act.activation(pT[:, n % 2, :, :], bank[6][:, 0:SEQ].rearrange("p (k n) -> p k n", k=2), ACT.Copy)\
                .then_inc(event("x_", "pT"), 1)
        merged_hi("m3_")
        conv(P_CO + 4, 4)
        conv(P_FI2, 4)
        sumsq(N_F2, x, xs_u, updated(U_CO + 2))
        rows1(N_F2, x, xs_u)
        features(N_F2, f_u, vt[:, V_FFN2:V_FFN2 + 8], None)
        feed_forward(P_FI2, U_FI2, "f2_", 0)
        sumsq(N_FINAL2, x, xs_u, updated(U_FI2 + 2))

    @block.vector
    def _(dve):
        def conv(p, n=1, i=0):
            for q in range(p, p + n):
                b, half = block_of(q)
                dve.wait_ge(hi_ready, q + 1 + i * 8)
                m = KD * SMALL if q == P_SMALL else PIECE
                dve.tensor_tensor(w_lo[:, q % RING, 0:m], raw[:, b % RAW, half * PIECE:half * PIECE + m],
                                  w_hi[:, q % RING, 0:m], ALU.subtract).then_inc(lo_ready, 1)

        def two(b):
            return bank[b][:].rearrange("p (k n) -> p k n", k=2)

        def mean(n):
            dve.wait_ge(nt["sumsq"], TT * (n + 1))
            dve.tensor_scalar(stat[:, 2:4], stat[:, 0:2], 1.0 / D, EPS, ALU.mult, ALU.add).then_inc(nt["mean"], 1)

        def rows0(n, src, dst):
            dve.wait_ge(nt["rstd"], n + 1)
            dve.tensor_scalar(dst[:, 0, :], src[:, 0, :], stat[:, 4:5], None, ALU.mult).then_inc(nt["rows0"], 1)

        def features(n, f, gain, shift, between=None):
            fi = F_OF[n]
            for g in (1, 3):
                dve.wait_ge(nt["turned"], 4 * fi + g + 1)
                for kk in range(2):
                    kt = 2 * g + kk
                    ps = bank[4 + g][:, kk * SEQ:(kk + 1) * SEQ]
                    if shift is None:
                        last = dve.tensor_scalar(f[:, kt, :], ps, gain[:, kt:kt + 1], None, ALU.mult)
                    else:
                        last = dve.tensor_scalar(f[:, kt, :], ps, gain[:, kt:kt + 1], shift[:, kt:kt + 1],
                                                 ALU.mult, ALU.add)
                last.then_inc(nt["feat_dve"], 1)
            for g in range(4):
                dve.wait_ge(nt["hi"], 4 * fi + g + 1)
                ks = slice(2 * g, 2 * g + 2)
                dve.tensor_tensor(a_lo[:, ks, :], f[:, ks, :], a_hi[:, ks, :], ALU.subtract).then_inc(nt["lo"], 1)
                if between is not None:
                    conv(between + g)

        def copy_pair(done, n, dst, b, copied):
            dve.wait_ge(done, n)
            dve.tensor_copy(dst, two(b)).then_inc(copied, 1)

        def ada_ops(k0, slab, slot, i=0, step=0):
            for k in (k0, k0 + 1):
                if k % 4 == 0:
                    dve.wait_ge(ada_landed[k // 4], 16 * (slab + 1) + i * (16 * step))
                w = ada_raw[:, k // 4, (k % 4) * W:(k % 4 + 1) * W]
                c = stat[:, 8 + k:9 + k]
                if k == 0:
                    o = dve.tensor_scalar(slot, w, c, None, ALU.mult)
                else:
                    dve.wait_ge(ada_step, 8 * slab + k + i * (8 * step))
                    o = dve.scalar_tensor_tensor(out=slot, in0=w, scalar=c, in1=slot, op0=ALU.mult, op1=ALU.add)
                o.then_inc(ada_step, 1)

        mean(N_MEM)
        rows0(N_MEM, mem_rows, xs_z)
        dve.wait_ge(sem["vec_turned"], 1)
        dve.tensor_copy(vt[:], bank[7][:, 0:V_ROWS]).then_inc(sem["vec_copied"], 1)
        dve.tensor_copy(taps[:].rearrange("p g k -> p (g k)"), bank[7][:, P:P + CG * TAPS]).then_inc(sem["vec_copied"], 1)
        dve.wait_ge(sem["vec_copied"], 2)
        features(N_MEM, f_z, vt[:, V_MEM:V_MEM + 8], None, P_CKV)
        for s in range(4):
            for k in range(4):
                if s == 0 and k == 0:
                    dve.wait_ge(sem["c_act"], 1)
                ada_ops(2 * k, s, ada_acc[:, s, :])
                if s < 3:
                    conv(P_CKV + 4 * s + 4 + k)
            if s == 3:
                conv(P_SMALL)
            dve.wait_ge(piece_used, P_CKV + 4 * s + 4)
            dst = k_rows if s < 2 else mem_v
            dve.tensor_copy(dst[:, 1, (s % 2) * W:(s % 2 + 1) * W], bank[2 * (s % 2) + 1][:]).then_inc(acc_free[1], 1)
            if s == 0:
                mean(N_H1)
                rows0(N_H1, x, xs_z)
            if s == 2:
                for g in (1, 3):
                    copy_pair(sem["key_turned"], g + 1, mem_kT[:, 2 * g:2 * g + 2, :], 4 + g, sem["key_copied"])
        dve.wait_ge(sem["ada_reduced"], 1)
        dve.tensor_tensor(modT[:, 0:16], bank[4][:, 0:16], vt[:, V_ADA:V_ADA + 16], ALU.add).then_inc(sem["mod_copied"], 1)
        dve.wait_ge(sem["mod_copied"], 1)
        dve.scalar_tensor_tensor(out=gain1[:], in0=modT[:, 8:16], scalar=1.0, in1=vt[:, V_MIX:V_MIX + 8],
                                 op0=ALU.add, op1=ALU.mult).then_inc(sem["gains"], 1)
        dve.wait_ge(sem["gains"], 1)
        features(N_H1, f_z, gain1, modT[:, 0:8])
        conv(P_IN1, 4)
        dve.wait_ge(piece_used, P_SMALL + 1)
        dve.tensor_copy(z[:, 1, C_KI:C_U], bank[2 * (U_SMALL % 2) + 1][:, 0:SMALL]).then_inc(acc_free[1], 1)

        def project_slabs(p, u, c0, n, ada=None, ada_slot=0):
            with dve.Fori(0, n // 2) as i:
                for s in range(2):
                    for k in range(4):
                        if ada is not None:
                            ada_ops(2 * k, ada + s, ada_acc[:, bass.ds(i * 2 + s, 1), :].rearrange("p o n -> p (o n)"),
                                    i, 2)
                        conv(p + 4 * s + 4 + k, 1, i)
                    dve.wait_ge(piece_used, p + 4 * s + 4 + i * 8)
                    dve.tensor_copy(z[:, 1, bass.ds(i * (2 * W) + (c0 + s * W), W)], bank[2 * ((u + s) % 2) + 1][:])\
                        .then_inc(acc_free[1], 1)

        project_slabs(P_IN1, U_IN1, 0, 4, 4)
        dve.wait_ge(sem["gate_bias_landed"], 32)

        def gate_rows(n, g, lo):
            dve.wait_ge(sem["ada_reduced"], n)
            for c in range(2):
                dve.tensor_tensor(g[:, c * W:(c + 1) * W], bank[5 + c][:], g[:, c * W:(c + 1) * W], ALU.add)
            dve.tensor_tensor(modT[:, lo:lo + 8], bank[4][:, 0:8], vt[:, V_ADA + lo:V_ADA + lo + 8], ALU.add)\
                .then_inc(sem["mod_copied"], 1)

        gate_rows(2, g_mix, 24)
        project_slabs(P_IN1 + 16, U_IN1 + 4, C_U, 4, 8)
        project_slabs(P_IN1 + 32, U_IN1 + 8, C_U + 4 * W, 2)
        gate_rows(3, g_ffn, 32)
        dve.wait_ge(sem["mod_copied"], 3)
        dve.scalar_tensor_tensor(out=gain2[:], in0=modT[:, 32:40], scalar=1.0, in1=vt[:, V_FFN:V_FFN + 8],
                                 op0=ALU.add, op1=ALU.mult).then_inc(sem["gains"], 1)

        dve.wait_ge(acc_free[0], U_IN1 + 10)
        dve.wait_ge(acc_free[1], U_IN1 + 10)
        for t in range(TT):
            for c in range(2):
                last = dve.tensor_copy(ki2[:, t, c, :], z[:, t, C_KI:C_WI])
        last.then_inc(sem["ki_copied"], 1)
        dve.tensor_scalar(wi_s[:], z[:, :, C_WI:C_U], HEADS ** -0.5, None, ALU.mult).then_inc(sem["wi_scaled"], 1)
        dve.memset(conv_in[:, :, 0:PAD], 0.0).then_inc(sem["pad_zeroed"], 1)
        copy_pair(sem["t1"], 2, qiT[:, 2:4, :], 5, sem["t1_copied_dve"])
        copy_pair(sem["t1"], 5, qT[:, 2:4, :], 1, sem["t1_copied_dve"])
        copy_pair(sem["t1"], 7, kT[:, 2:4, :], 3, sem["t1_copied_dve"])
        dve.wait_ge(sem["wi_scaled"], 1)
        for n in range(TT * HEADS):
            t, h = n // HEADS, n % HEADS
            keys = P * (t + 1)
            dve.wait_ge(sem["relu_done"], n + 1)
            if n:
                dve.wait_ge(sem["score_step"], n)
            add = C("causal", SEQ - keys) if h == 0 else score[:, t, 0:keys]
            dve.scalar_tensor_tensor(out=score[:, t, 0:keys], in0=relu_t[:, n % 2, 0:keys], scalar=wi_s[:, t, h:h + 1],
                                     in1=add, op0=ALU.mult, op1=ALU.add).then_inc(sem["score_step"], 1)
        step = 0
        for t in range(TT):
            keys = P * (t + 1)
            row = score[:, t, 0:keys]
            dve.wait_ge(sem["score_step"], TT * HEADS)
            for r in range(TOPK // 8):
                if step:
                    dve.wait_ge(sem["top_step"], step)
                dve.max(top8[:], row).then_inc(sem["top_step"], 1)
                dve.wait_ge(sem["top_step"], step + 1)
                dve.match_replace(row, top8[:], row, TAKEN).then_inc(sem["top_step"], 1)
                step += 2
            dve.wait_ge(sem["top_step"], step)
            dve.tensor_scalar(row, row, -2e38, -8e30, ALU.is_gt, ALU.mult).then_inc(sem["top_step"], 1)
            dve.wait_ge(sem["top_step"], step + 1)
            dve.tensor_tensor(row, row, C("causal", SEQ - keys), ALU.add).then_inc(sem["top_step"], 1)
            step += 2
        for t in range(TT):
            dve.wait_ge(sem["sig_u"], t + 1)
            dve.tensor_tensor(z[:, t, C_U:C_U + W], z[:, t, C_U:C_U + W], z[:, t, C_U + W:C_U + 2 * W], ALU.mult)\
                .then_inc(sem["glu"], 1)
        dve.wait_ge(sem["conv_turned"], 2)
        dve.tensor_copy(conv_in[:, 2:4, PAD:], two(7)).then_inc(sem["conv_in_dve"], 1)

        def softmax_steps(tag, bias_of, steps=STEPS):
            for n, (h, t) in enumerate(steps):
                keys = P * (t + 1)
                bias = bias_of(n, h, t, keys)
                dve.wait_ge(*after(tag, "scores", n + 1))
                if n >= 2:
                    dve.wait_ge(*after(tag, "exp", n - 1))
                dve.tensor_tensor_reduce(s_work[:, n % 2, 0, 0:keys], bank[4 + n % 2][:, 0:keys], bias, DH ** -0.5,
                                         -3e38, ALU.add, ALU.max, stat[:, 32 + n % 2:33 + n % 2])\
                    .then_inc(event(tag, "max"), 1)
                dve.wait_ge(*after(tag, "max", n + 1))
                dve.tensor_scalar(stat[:, 34 + n % 2:35 + n % 2], stat[:, 32 + n % 2:33 + n % 2], -1.0, None, ALU.mult)\
                    .then_inc(event(tag, "negmax"), 1)

        def selected_bias(n, h, t, keys):
            if n:
                dve.wait_ge(*after("a1_", "max", n))
            dve.scalar_tensor_tensor(out=bias_t[:, 0:keys], in0=C("rel", SEQ - keys), scalar=2.0 ** -(h + 1),
                                     in1=score[:, t, 0:keys], op0=ALU.mult, op1=ALU.add).then_inc(event("a1_", "bias"), 1)
            dve.wait_ge(*after("a1_", "bias", n + 1))
            return bias_t[:, 0:keys]

        dve.wait_ge(sem["top_step"], step)
        softmax_steps("a1_", selected_bias)

        def head_outputs(tag, n_steps, heads, banks_of, dst, done):
            dve.wait_ge(*after(tag, "exp", n_steps))
            dve.reciprocal(stat[:, 36:36 + TT * heads], stat[:, 36:36 + TT * heads]).then_inc(event(tag, "recip"), 1)
            dve.wait_ge(*after(tag, "recip", 1))
            dve.wait_ge(*after(tag, "pv", n_steps))
            per = heads // len(banks_of(0))
            for k in range(len(banks_of(0))):
                for t in range(TT):
                    b = banks_of(t)[k]
                    r = stat[:, 36 + t * heads + k * per:36 + t * heads + (k + 1) * per]
                    o = dve.tensor_tensor(dst[:, t, k * W:(k + 1) * W].rearrange("p (h d) -> p h d", h=per),
                                          bank[b][:].rearrange("p (h d) -> p h d", h=per),
                                          r.unsqueeze(2).to_broadcast([P, per, W // per]), ALU.mult)
                    o.then_inc(done, 1)

        head_outputs("a1_", 16, HEADS, lambda t: [t], y_rows, sem["y1"])

        dve.wait_ge(sem["conv_in_act"], 1)
        dve.wait_ge(sem["conv_in_dve"], 1)
        for g in range(CG):
            dve.tensor_scalar(conv_out[:, g, :], conv_in[:, g, 0:SEQ], taps[:, g, 0:1], vt[:, V_BDW + g:V_BDW + g + 1],
                              ALU.mult, ALU.add).then_inc(sem["conv_done"], 1)
        with dve.Fori(0, TAPS - 1) as i:
            for g in range(CG):
                dve.wait_ge(sem["conv_done"], g + 1 + i * 4)
                dve.scalar_tensor_tensor(out=conv_out[:, g, :], in0=conv_in[:, g, bass.ds(i + 1, SEQ)],
                                         scalar=taps[:, g, bass.ds(i + 1, 1)], in1=conv_out[:, g, :],
                                         op0=ALU.mult, op1=ALU.add).then_inc(sem["conv_done"], 1)
        dve.wait_ge(sem["ln_mean"], 1)
        dve.tensor_tensor(conv_out[:], conv_out[:], bank[4][:, 0:SEQ].unsqueeze(1).to_broadcast([P, CG, SEQ]),
                          ALU.subtract).then_inc(sem["ln_centred"], 1)
        dve.wait_ge(sem["ln_centred"], 1)
        dve.tensor_tensor(conv_sq[:], conv_out[:], conv_out[:], ALU.mult).then_inc(sem["ln_square"], 1)
        dve.wait_ge(sem["ln_sumsq"], 1)
        dve.tensor_scalar(conv_sq[:, 0, :], bank[5][:, 0:SEQ], EPS, None, ALU.add).then_inc(sem["ln_var"], 1)
        dve.wait_ge(sem["ln_rstd"], 1)
        dve.tensor_tensor(conv_out[:], conv_out[:], conv_sq[:, 1, :].unsqueeze(1).to_broadcast([P, CG, SEQ]),
                          ALU.mult).then_inc(sem["ln_scaled"], 1)
        dve.wait_ge(sem["conv_hi"], 1)
        dve.tensor_tensor(a_lo[:, 4:8, :], conv_in[:, :, 0:SEQ], a_hi[:, 4:8, :], ALU.subtract).then_inc(sem["conv_lo"], 1)
        for g in range(2):
            dve.wait_ge(sem["y1_hi"], g + 1)
            dve.tensor_tensor(a_lo[:, 2 * g:2 * g + 2, :], two(6 + g), a_hi[:, 2 * g:2 * g + 2, :], ALU.subtract)\
                .then_inc(sem["y1_lo"], 1)

        def gated_halves(p1, p2, u, gates, c_a, c_b, tag):
            dve.wait_ge(gates, TT)
            step = 0
            for c in range(2):
                conv(p2 + 2 * c, 2)
                dve.wait_ge(piece_used, p1 + 2 * c + 2)
                for t in range(TT):
                    dve.tensor_tensor(z[:, t, c * W:(c + 1) * W], bank[2 * ((u + c) % 2) + t][:],
                                      z[:, t, c_a + c * W:c_a + (c + 1) * W], ALU.mult).then_inc(acc_free[t], 1)
            for c in range(2):
                conv(p2 + 4 + 2 * c, 2)
                dve.wait_ge(piece_used, p2 + 2 * c + 2)
                for t in range(TT):
                    step += 1
                    dve.tensor_tensor(z[:, t, c_b + c * W:c_b + (c + 1) * W], bank[2 * ((u + 2 + c) % 2) + t][:],
                                      z[:, t, c_b + c * W:c_b + (c + 1) * W], ALU.mult).then_inc(acc_free[t], 1)
                    dve.wait_ge(acc_free[t], u + 2 + c + 1)
                    dve.tensor_tensor(z[:, t, c * W:(c + 1) * W], z[:, t, c * W:(c + 1) * W],
                                      z[:, t, c_b + c * W:c_b + (c + 1) * W], ALU.add).then_inc(event(tag, "merged"), 1)

        def merged_lo(tag):
            for g in range(4):
                dve.wait_ge(*after(tag, "hi", g + 1))
                dve.tensor_tensor(a_lo[:, 2 * g:2 * g + 2, :], two(4 + g), a_hi[:, 2 * g:2 * g + 2, :], ALU.subtract)\
                    .then_inc(event(tag, "lo"), 1)

        def residual(t, c, b, gate, done):
            xs, src = x[:, t, c * W:(c + 1) * W], bank[b][:]
            if gate is not None:
                tmp = tmp_rows[:, gated[0] % 2, :]
                dve.tensor_tensor(tmp, src, gate[:, c * W:(c + 1) * W], ALU.mult)\
                    .then_inc(sem["gated"], 1)
                gated[0] += 1
                dve.wait_ge(sem["gated"], gated[0])
                src = tmp
            dve.tensor_tensor(xs, src, xs, ALU.add).then_inc(done, 1)

        gated = [0]

        def project_out(p, u, gate, tag):
            for s in range(2):
                conv(p + 4 * s + 4, 4)
                dve.wait_ge(piece_used, p + 4 * s + 4)
                for t in range(TT):
                    residual(t, s, 2 * ((u + s) % 2) + t, gate, acc_free[t])

        gated_halves(P_PA, P_PC, U_PA, sem["sig_gates"], C_GA, C_GB, "m1_")
        merged_lo("m1_")
        project_out(P_OUT1, U_OUT1, g_mix, "m1_")
        mean(N_H2)
        rows0(N_H2, x, xs_u)
        features(N_H2, f_u, gain2, modT[:, 24:32])

        def feed_forward(p, u, tag, gate, following):
            def hidden(s, i=0):
                for t in range(TT):
                    dve.wait_ge(*after(tag, "silu", TT * s + t + 1 + i * 4))
                    dve.tensor_tensor(ff_hid[:, t, :], bank[2 * ((u + s) % 2) + t][:, GW:2 * GW], ff_act[:, t, :],
                                      ALU.mult).then_inc(event(tag, "hidden"), 1)

            def hidden_lo(s, ks, i=0):
                dve.wait_ge(*after(tag, "hidden_hi", s + 1 + i * 2))
                dve.tensor_tensor(f_lo[:, ks, :], two(4 + s % 2), f_hi[:, ks, :], ALU.subtract)\
                    .then_inc(event(tag, "hidden_lo"), 1)

            conv(p + 4, 4)
            with dve.Fori(0, 5) as i:
                for s in (1, 2):
                    hidden(s - 1, i)
                    conv(p + 4 * s + 4, 2, i)
                    hidden_lo(s - 1, bass.ds(i * 4 + (2 * s - 2), 2), i)
                    conv(p + 4 * s + 6, 2, i)
            last = NSLAB_FF - 1
            hidden(last)
            p += 4 * NSLAB_FF
            conv(p + 4, 2)
            hidden_lo(last, slice(2 * last, 2 * last + 2))
            with dve.Fori(0, 2) as i:
                conv(p + 6, 8, i)
            conv(p + KF, following)
            dve.wait_ge(piece_used, p + KF)
            for t in range(TT):
                for c in range(2):
                    residual(t, c, 2 * t + c, gate, acc_free[t])

        def final_norm(n, landed, done):
            mean(n)
            dve.wait_ge(final_landed, landed)
            dve.wait_ge(nt["rstd"], n + 1)
            for t in range(TT):
                dve.scalar_tensor_tensor(out=x[:, t, :], in0=x[:, t, :], scalar=stat[:, 4 + t:5 + t], in1=final_g[:],
                                         op0=ALU.mult, op1=ALU.mult).then_inc(done, 1)

        feed_forward(P_FI1, U_FI1, "f1_", g_ffn, 4)
        final_norm(N_FINAL1, 16, sem["final1_done"])
        mean(N_M2)
        rows0(N_M2, x, xs_u)
        features(N_M2, f_u, vt[:, V_MIX2:V_MIX2 + 8], None)
        project_slabs(P_IN2, U_IN2, 0, 10)

        dve.wait_ge(acc_free[0], U_IN2 + 10)
        dve.wait_ge(acc_free[1], U_IN2 + 10)
        step = 0
        for t in range(TT):
            heads = z[:, t, E_QA:E_VA].rearrange("p (h d) -> p h d", d=DH)
            turned = xs_u[:, t, :].rearrange("p (h d) -> p h d", d=DH)
            cs = C("cos", t * DH, (t + 1) * DH).unsqueeze(1).to_broadcast([P, 16, DH])
            sn_lo = C("sin", t * DH, t * DH + 32).unsqueeze(1).to_broadcast([P, 16, 32])
            sn_hi = C("sin", t * DH + 32, (t + 1) * DH).unsqueeze(1).to_broadcast([P, 16, 32])
            dve.tensor_tensor(turned[:, :, 0:32], heads[:, :, 32:64], sn_lo, ALU.mult)
            dve.tensor_tensor(turned[:, :, 32:64], heads[:, :, 0:32], sn_hi, ALU.mult).then_inc(sem["rope"], 1)
            dve.wait_ge(sem["rope"], t + 1)
            dve.tensor_tensor(heads, heads, cs, ALU.mult).then_inc(sem["rope_cos"], 1)
            dve.wait_ge(sem["rope_cos"], t + 1)
            dve.tensor_tensor(heads, heads, turned, ALU.add).then_inc(sem["rope_sum"], 1)
        copy_pair(sem["t2"], 2, qbT[:, 2:4, :], 5, sem["t2_copied_dve"])
        copy_pair(sem["t2"], 4, kbT[:, 2:4, :], 7, sem["t2_copied_dve"])
        dve.wait_ge(late_landed, 64)
        for c in range(2):
            dve.tensor_tensor_reduce(tmp_rows[:, 0, c * DH:(c + 1) * DH], lam[:, 2 * c, :], lam[:, 2 * c + 1, :], 1.0, 0.0, ALU.mult, ALU.add,
                                     stat[:, 54 + c:55 + c]).then_inc(sem["lam_dots"], 1)
        copy_pair(sem["t2"], 6, qaT[:, 2:4, :], 1, sem["t2_copied_dve"])
        copy_pair(sem["t2"], 8, kaT[:, 2:4, :], 3, sem["t2_copied_dve"])
        dve.wait_ge(sem["lam_exp"], 1)
        dve.scalar_tensor_tensor(out=stat[:, 58:59], in0=stat[:, 56:57], scalar=0.8 - 0.6, in1=stat[:, 57:58],
                                 op0=ALU.add, op1=ALU.subtract).then_inc(sem["lambda"], 1)

        def band_bias(n, h, t, keys):
            if t == 0:
                if n:
                    dve.wait_ge(*after("b_", "max", n))
                dve.scalar_tensor_tensor(out=bias_t[:], in0=rel_rows[:, h, ::-1], scalar=8.0, in1=C("chunk"),
                                         op0=ALU.mult, op1=ALU.add).then_inc(event("b_", "bias"), 1)
                dve.wait_ge(*after("b_", "bias", h + 1))
            return bias_t[:, SEQ - keys:]

        dve.wait_ge(sem["rel_landed"], 16)
        softmax_steps("b_", band_bias)
        head_outputs("b_", 16, HEADS, lambda t: [t], y2_rows, sem["yb"])
        dve.wait_ge(sem["lambda"], 1)
        for n in range(8):
            h, t = n // 2, n % 2
            keys = P * (t + 1)
            par = n % 2

            def d_mix(m):
                q = m % 2
                ks = P * (m % 2 + 1)
                dve.wait_ge(*after("d_", "exp", 2 * m + 2))
                dve.reciprocal(d_stat[:, 12 + 2 * q:14 + 2 * q], d_stat[:, 8 + 2 * q:10 + 2 * q]).then_inc(event("d_", "recip"), 1)
                dve.wait_ge(*after("d_", "recip", 2 * m + 1))
                dve.tensor_tensor(d_stat[:, 16 + q:17 + q], d_stat[:, 13 + 2 * q:14 + 2 * q], stat[:, 58:59], ALU.mult)\
                    .then_inc(event("d_", "recip"), 1)
                dve.wait_ge(*after("d_", "recip", 2 * m + 2))
                dve.tensor_scalar(p_work[:, q, 1, 0:ks], p_work[:, q, 1, 0:ks], d_stat[:, 16 + q:17 + q], None, ALU.mult)\
                    .then_inc(event("d_", "second"), 1)
                dve.wait_ge(*after("d_", "second", m + 1))
                dve.scalar_tensor_tensor(out=p_work[:, q, 0, 0:ks], in0=p_work[:, q, 0, 0:ks],
                                         scalar=d_stat[:, 12 + 2 * q:13 + 2 * q], in1=p_work[:, q, 1, 0:ks],
                                         op0=ALU.mult, op1=ALU.subtract).then_inc(event("d_", "mix"), 1)

            dve.wait_ge(*after("d_", "scores", n + 1))
            if n >= 2:
                dve.wait_ge(*after("d_", "exp", 2 * (n - 1)))
            for c in range(2):
                last = dve.tensor_tensor_reduce(s_work[:, par, c, 0:keys], bank[D_BANKS[par][c]][:, 0:keys],
                                                C("chunk", SEQ - keys), DH ** -0.5, -3e38, ALU.add, ALU.max,
                                                d_stat[:, 2 * par + c:2 * par + c + 1])
            last.then_inc(event("d_", "max"), 1)
            dve.wait_ge(*after("d_", "max", n + 1))
            dve.tensor_scalar(d_stat[:, 4 + 2 * par:6 + 2 * par], d_stat[:, 2 * par:2 * par + 2], -1.0, None, ALU.mult)\
                .then_inc(event("d_", "negmax"), 1)
            if n >= 1:
                d_mix(n - 1)
        d_mix(7)
        dve.wait_ge(*after("d_", "pv", 8))
        for t in range(TT):
            for h in range(4):
                ps = bank[2 + t][:, h * P:(h + 1) * P]
                last = dve.tensor_copy(z[:, t, h * P:(h + 1) * P], ps)
            last.then_inc(sem["ya_rows"], 1)
        dve.wait_ge(sem["ya_rows"], TT)
        for t in range(TT):
            for h in range(4):
                r = z[:, t, h * P:(h + 1) * P]
                last = dve.tensor_tensor_reduce(tmp_rows[:, t, h * P:(h + 1) * P], r, r, 1.0, 0.0, ALU.mult, ALU.add,
                                                d_stat[:, 20 + 4 * t + h:21 + 4 * t + h])
        last.then_inc(sem["ya_sumsq"], 1)
        dve.wait_ge(sem["ya_sumsq"], 1)
        dve.tensor_scalar(stat[:, 16:24], d_stat[:, 20:28], 1.0 / P, EPS, ALU.mult, ALU.add).then_inc(sem["sub_mean"], 1)
        dve.wait_ge(sem["sub_rstd"], 1)
        for t in range(TT):
            r = z[:, t, 0:W].rearrange("p (h d) -> p h d", h=4)
            dve.tensor_tensor(r, r, stat[:, 24 + 4 * t:28 + 4 * t].unsqueeze(2).to_broadcast([P, 4, P]), ALU.mult)\
                .then_inc(sem["ya"], 1)
        for g in range(2):
            dve.wait_ge(sem["y2_turned"], g + 1)
            dve.tensor_scalar(f_u[:, 2 * g:2 * g + 2, :], two(4 + g), vt[:, V_SUB:V_SUB + 1], 1.0 - (0.8 - 0.6),
                              ALU.mult, ALU.mult).then_inc(sem["ya_feat"], 1)
        for g in range(2):
            dve.wait_ge(sem["y2_hi"], g + 1)
            dve.tensor_tensor(a_lo[:, 2 * g:2 * g + 2, :], f_u[:, 2 * g:2 * g + 2, :], a_hi[:, 2 * g:2 * g + 2, :],
                              ALU.subtract).then_inc(sem["y2_lo"], 1)
        for g in range(2):
            dve.wait_ge(sem["y2_hi"], 3 + g)
            dve.tensor_tensor(a_lo[:, 4 + 2 * g:6 + 2 * g, :], two(6 + g), a_hi[:, 4 + 2 * g:6 + 2 * g, :],
                              ALU.subtract).then_inc(sem["y2_lo"], 1)
        gated_halves(P_UA, P_UB, U_UA, sem["sig_gates2"], E_GA, E_GB, "m2_")
        merged_lo("m2_")
        project_out(P_OUT2, U_OUT2, None, "m2_")
        mean(N_CR)
        rows0(N_CR, x, xs_u)
        features(N_CR, f_u, vt[:, V_CROSS:V_CROSS + 8], None)

        for s in range(2):
            conv(P_CQ + 4 + 4 * s, 4)
            dve.wait_ge(piece_used, P_CQ + 4 * s + 4)
            dve.tensor_copy(qx_rows[:, 1, s * W:(s + 1) * W], bank[2 * ((U_CQ + s) % 2) + 1][:]).then_inc(acc_free[1], 1)
        for g in (1, 3):
            copy_pair(sem["qx_turned"], g + 1, qxT[:, 2 * g:2 * g + 2, :], 4 + g, sem["qx_copied_dve"])
        for n in range(8):
            dve.wait_ge(*after("x_", "scores", n + 1))
            if n >= 2:
                dve.wait_ge(*after("x_", "exp", n - 1))
            dve.tensor_reduce(stat[:, 32 + n % 2:33 + n % 2], bank[4 + n % 2][:, 0:SEQ], AX_X, ALU.max)\
                .then_inc(event("x_", "max"), 1)
            dve.wait_ge(*after("x_", "max", n + 1))
            dve.tensor_scalar(stat[:, 34 + n % 2:35 + n % 2], stat[:, 32 + n % 2:33 + n % 2], -1.0 / 16, None, ALU.mult)\
                .then_inc(event("x_", "negmax"), 1)
        head_outputs("x_", 8, 4, lambda t: [t, 2 + t], merged, event("m3_", "merged"))
        merged_lo("m3_")
        project_out(P_CO, U_CO, None, "m3_")
        mean(N_F2)
        rows0(N_F2, x, xs_u)
        features(N_F2, f_u, vt[:, V_FFN2:V_FFN2 + 8], None)
        feed_forward(P_FI2, U_FI2, "f2_", None, 0)
        final_norm(N_FINAL2, 32, sem["result"])

    ctx.close()


_INS = ["x", "c", "norm_mix_g", "w_in", "w_dw", "b_dw", "conv_ln_g", "conv_ln_b", "w_attn_proj", "w_conv_proj", "w_out",
        "norm_ffn_g", "w_ffn_in", "w_ffn_out", "w_ada", "b_ada", "norm_final_g", "mem_2", "norm_mix_g_2", "w_in_2",
        "lam_q1_2", "lam_k1_2", "lam_q2_2", "lam_k2_2", "subln_g_2", "rel_bias_2", "w_up_a_2", "w_up_b_2", "w_out_2",
        "norm_cross_g_2", "norm_mem_g_2", "w_cq_2", "w_ckv_2", "w_co_2", "norm_ffn_g_2", "w_gate_up_2", "w_down_2",
        "norm_final_g_2"]


def kernel(**inputs):
    import numpy as _np
    import concourse.bacc as _bacc
    from concourse.bass_utils import run_bass_kernel_spmd as _run

    nc = _bacc.Bacc("TRN2", target_bir_lowering=False, num_devices=1)
    arrays, args = {}, {}
    for name in _INS:
        v = _np.ascontiguousarray(inputs[name])
        arrays[f"in_{name}"] = v
        args[name] = nc.dram_tensor(f"in_{name}", v.shape, mybir.dt.from_np(v.dtype), kind="ExternalInput").ap()
    out = nc.dram_tensor("out_x", (1, SEQ, D), F32, kind="ExternalOutput").ap()
    build(nc, args, out)
    r = _run(nc, [arrays], core_ids=[0])
    return r.results[0]["out_x"]
```

```python
from contextlib import ExitStack

import concourse.bass as bass
from concourse import mybir
from concourse.alu_op_type import AluOpType as ALU

F32 = mybir.dt.float32
F32R = mybir.dt.float32r
ACT = mybir.ActivationFunctionType
AX_X = mybir.AxisListType.X

P = 128
SEQ = 256
TT = SEQ // P
D = 1024
KD = D // P
W = 512
DFF = 2816
KF = DFF // P
GW = 256
NSLAB_FF = DFF // GW
EPS = 1e-6
HEADS, DH = 8, 64
TOPK = 64
TAPS = 31
PAD = TAPS - 1
CG = 4
NEG = -1e38
TAKEN = -3e38
BLK = 2048
PIECE = 1024
RAW = 4
RING = 4
IN1 = 5192
IN2 = 5120
C_Q, C_K, C_V, C_QI, C_KI, C_WI, C_U, C_GA, C_GB = 0, 512, 1024, 1536, 2048, 2112, 2120, 3144, 4168
E_QA, E_KA, E_VA, E_QB, E_KB, E_VB, E_GA, E_GB = 0, 512, 1024, 1536, 2048, 2560, 3072, 4096
SMALL = C_U - C_KI


def constants(np):
    parts = {}
    i = np.arange(P)
    parts["ident"] = np.eye(P)
    parts["ones"] = np.ones((P, P))
    parts["mean512"] = np.full((P, P), 1.0 / 512)
    rel = i[None, :] - i[:, None]
    parts["rel"] = np.concatenate([rel - P, rel], 1) * 8.0
    parts["causal"] = np.concatenate([np.zeros((P, P)), np.where(rel <= 0, 0.0, NEG)], 1)
    late = (i[None, :] // 64) > (i[:, None] // 64)
    parts["chunk"] = np.concatenate([np.zeros((P, P)), np.where(late, -8e30, 0.0)], 1)
    inv = 1.0 / (10000.0 ** (np.arange(0, 64, 2, dtype=np.float32) / np.float32(64)))
    ang = np.arange(SEQ, dtype=np.float32)[:, None] * inv.astype(np.float32)[None, :]
    cos, sin = np.cos(ang).astype(np.float32), np.sin(ang).astype(np.float32)
    parts["cos"] = np.concatenate([cos, cos], 1).reshape(TT, P, 64).transpose(1, 0, 2).reshape(P, TT * 64)
    parts["sin"] = np.concatenate([-sin, sin], 1).reshape(TT, P, 64).transpose(1, 0, 2).reshape(P, TT * 64)
    parts["half"] = np.full((P, KD), -0.5)
    at, n = {}, 0
    for name, a in parts.items():
        at[name] = (n, n + a.shape[1])
        n += a.shape[1]
    return np.ascontiguousarray(np.concatenate(list(parts.values()), 1).astype(np.float32)), at


P_CKV, U_CKV = 0, 0
P_SMALL, U_SMALL = 16, 4
P_IN1, U_IN1 = 17, 5
P_PA, U_PA = 57, 15
P_PC, U_PC = 61, 17
P_OUT1, U_OUT1 = 65, 19
P_FI1, U_FI1 = 73, 21
P_FO1, U_FO1 = 117, 21
P_IN2, U_IN2 = 139, 23
P_UB, U_UB = 179, 33
P_UA, U_UA = 183, 35
P_OUT2, U_OUT2 = 187, 37
P_CQ, U_CQ = 195, 39
P_CO, U_CO = 203, 41
P_FI2, U_FI2 = 211, 43
P_FO2, U_FO2 = 255, 43
P_END = 277
B_END = 9 + (P_END - 17) // 2


def block_of(p):
    if p < 16:
        return p // 2, p % 2
    if p == 16:
        return 8, 0
    return 9 + (p - 17) // 2, (p - 17) % 2


def pair_blocks(b):
    pairs = [q for p in (P_FI1, P_FI2) for q in range(block_of(p)[0], block_of(p)[0] + 2 * NSLAB_FF + 2)]
    return sum(q <= b and q % RAW == b % RAW for q in pairs) if b in pairs else 0


def last_piece_of(b):
    return 2 * b + 1 if b < 8 else 16 if b == 8 else 17 + 2 * (b - 9) + 1


N_MEM, N_H1, N_H2, N_FINAL1, N_M2, N_CR, N_F2, N_FINAL2 = range(8)
F_OF = {N_MEM: 0, N_H1: 1, N_H2: 2, N_M2: 3, N_CR: 4, N_F2: 5}
V_C, V_MIX, V_FFN, V_MIX2, V_CROSS, V_MEM, V_FFN2, V_CLG, V_CLB, V_BDW, V_SUB, V_ADA = \
    0, 8, 16, 24, 32, 40, 48, 56, 60, 64, 68, 69
V_ROWS = V_ADA + 48


def build(nc, a, out):
    import numpy as np

    table, cols = constants(np)
    const_dram = nc.inline_tensor(table, name="shape_constants")

    cursor = [16512]

    def region(nbytes):
        at = cursor[0]
        cursor[0] += (nbytes + 31) // 32 * 32
        return at

    def sb(name, shape, dtype=F32, at=None):
        n = 4
        for s in shape[1:]:
            n *= s
        return nc.alloc_sbuf_tensor_at(name, shape, dtype, offset=region(n) if at is None else at)

    raw = sb("raw_weights", [P, RAW, BLK])
    w_hi = sb("w_hi", [P, RING, PIECE], F32R)
    w_lo = sb("w_lo", [P, RING, PIECE], F32R)
    a_hi = sb("a_hi", [P, KD, SEQ], F32R)
    a_lo = sb("a_lo", [P, KD, SEQ], F32R)
    x = sb("x_residual", [P, TT, D])
    z_at = region(2 * KF * SEQ * 4)
    z = sb("z_projected", [P, TT, IN1], at=z_at)
    xs_z = sb("scaled_rows_early", [P, TT, D], at=z_at)
    f_z = sb("feature_rows_early", [P, KD, SEQ], at=z_at + 8192)
    mem_rows = sb("mem_rows", [P, TT, D], at=z_at + 16384)
    k_rows = sb("mem_key_rows", [P, TT, D], at=z_at + 24576)
    f_hi = sb("ff_hi", [P, KF, SEQ], F32R, at=z_at)
    f_lo = sb("ff_lo", [P, KF, SEQ], F32R, at=z_at + KF * SEQ * 4)
    mem_kT = sb("mem_kT", [P, KD, SEQ])
    mem_v = sb("mem_v", [P, TT, D])
    g_mix = sb("gate_mix_rows", [P, D])
    g_ffn = sb("gate_ffn_rows", [P, D])
    final_g = sb("final_gain_rows", [P, D])
    const = sb("constants", [P, table.shape[1]])

    def C(name, lo=0, hi=None):
        c0, c1 = cols[name]
        return const[:, c0 + lo:(c1 if hi is None else c0 + hi)]

    ident, ones, mean512 = C("ident"), C("ones"), C("mean512")
    vt = sb("vectors_T", [P, V_ROWS])
    modT = sb("modulation_T", [P, 48])
    gain1 = sb("gain_h1", [P, KD])
    gain2 = sb("gain_h2", [P, KD])
    taps = sb("conv_taps_T", [P, CG, TAPS])
    stat = sb("row_stats", [P, 64])
    d_stat = sb("component_stats", [P, 32])
    top8 = sb("top8", [P, 8])
    wi_s = sb("index_weights", [P, TT, HEADS])
    lam = sb("lambda_parts", [P, 4, 64])
    u_at = region(24576)
    xs_u = sb("scaled_rows", [P, TT, D], at=u_at)
    f_u = sb("feature_rows", [P, KD, SEQ], at=u_at + 8192)
    ada_raw = sb("ada_raw", [P, 2, BLK], at=u_at)
    vec_rows = sb("vector_rows", [P, P], at=u_at + 16384)
    tap_rows = sb("tap_rows", [TAPS, W], at=u_at + 16384 + 512)
    qT = sb("qT", [P, CG, SEQ], at=u_at)
    kT = sb("kT", [P, CG, SEQ], at=u_at + 4096)
    qiT = sb("qiT", [P, CG, SEQ], at=u_at + 8192)
    kiT = sb("kiT", [P, SEQ], at=u_at + 12288)
    ki2 = sb("ki_twice", [P, TT, 2, DH], at=u_at + 13312)
    conv_in = sb("conv_in", [P, CG, PAD + SEQ], at=u_at + 14336)
    conv_out = sb("conv_out", [P, CG, SEQ], at=u_at + 14336 + 4576)
    conv_sq = sb("conv_sq", [P, CG, SEQ], at=u_at + 8192)
    qaT = sb("qaT", [P, CG, SEQ], at=u_at)
    kaT = sb("kaT", [P, CG, SEQ], at=u_at + 4096)
    qbT = sb("qbT", [P, CG, SEQ], at=u_at + 8192)
    kbT = sb("kbT", [P, CG, SEQ], at=u_at + 12288)
    rel_rows = sb("rel_bias_rows", [P, HEADS, SEQ], at=u_at + 16384)
    qxT = sb("qxT", [P, KD, SEQ], at=u_at)
    qx_rows = sb("qx_rows", [P, TT, D], at=u_at + 8192)
    w_at = region(13 * 1024)
    ada_acc = sb("ada_acc", [P, 6, W], at=w_at)
    score = sb("score", [P, TT, SEQ], at=z_at + TT * IN1 * 4)
    s_work = sb("masked_scores", [P, 2, 2, SEQ], at=w_at + 2048)
    p_work = sb("probabilities", [P, 2, 2, SEQ], at=w_at + 6144)
    pT = sb("probabilities_T", [P, 2, TT, P], at=w_at + 10240)
    bias_t = sb("bias_tile", [P, SEQ], at=w_at + 12288)
    relu_t = sb("relu_tile", [P, 2, SEQ], at=z_at + C_GB * 4)
    ff_act = sb("silu_rows", [P, TT, GW], at=w_at)
    ff_hid = sb("hidden_rows", [P, TT, GW], at=w_at + 2048)
    tmp_rows = sb("tmp_rows", [P, TT, W], at=w_at + 4096)
    assert cursor[0] <= 229344, cursor[0]
    y_rows = z[:, :, 0:W]
    y2_rows = z[:, :, W:2 * W]
    merged = z[:, :, 0:D]

    bank = [nc.alloc_psum_tensor(f"bank{i}", [P, W], F32) for i in range(8)]

    def S(name):
        return nc.alloc_semaphore(name)

    raw_landed = [S(f"raw_landed{i}") for i in range(RAW)]
    second_landed = [S(f"second_half_landed{i}") for i in range(RAW)]
    hi_ready, lo_ready, piece_used = S("hi_ready"), S("lo_ready"), S("piece_used")
    acc_free = [S("acc0_free"), S("acc1_free")]
    small_landed = S("small_landed")
    late_landed = S("late_landed")
    final_landed = S("final_landed")
    ada_landed = [S("ada_landed0"), S("ada_landed1")]
    ada_step = S("ada_step")
    nt = {k: S("norm_" + k) for k in ("sumsq", "mean", "rstd", "rows0", "rows1", "turned", "feat_act",
                                      "feat_dve", "hi", "lo")}
    out_done = S("out_done")

    class Named:

        def __init__(self):
            self.made = {}

        def __getitem__(self, name):
            if name not in self.made:
                self.made[name] = S(name)
            return self.made[name]

    sem = Named()
    FAMILIES = [("attention", ("a1_", "b_", "d_", "x_"),
                 {n: (16, 16, 8, 8) for n in ("scores", "negmax", "turned", "pT", "pv")}
                 | {"max": (16, 16, 16, 8), "exp": (16, 16, 16, 8), "bias": (16, 8, 0, 0), "recip": (1, 1, 16, 1)}),
                ("projection", ("m1_", "m2_", "m3_"),
                 {n: (4, 4, 4) for n in ("merged", "merged_turned", "hi", "lo")}),
                ("feed_forward", ("f1_", "f2_"),
                 {n: (2 * NSLAB_FF,) * 2 for n in ("silu", "hidden")}
                 | {n: (NSLAB_FF,) * 2 for n in ("hidden_turned", "hidden_hi", "hidden_lo")})]

    D_BANKS = (4, 5, 7)

    def family(tag):
        return next(f for f in FAMILIES if tag in f[1])

    def event(tag, name):
        kind, _, counts = family(tag)
        return sem[kind + "_" + name] if name in counts else sem[tag + name]

    def after(tag, name, value):
        _, tags, counts = family(tag)
        base = sum(counts[name][:tags.index(tag)]) if name in counts else 0
        return event(tag, name), base + value

    def updated(count):
        return lambda t: (acc_free[t], count)

    def slab_src(wt, k0, c0):
        return wt.rearrange("(k p) n -> p k n", p=P)[:, k0:k0 + 4, c0:c0 + W] if isinstance(c0, int) else \
            wt.rearrange("(k p) n -> p k n", p=P)[:, k0:k0 + 4, bass.ds(c0, W)]

    def pair_src(wt, k0, j):
        v = wt.rearrange("(k p) (h n) -> p k h n", p=P, h=2)
        return [v[:, k0:k0 + 4, h, bass.ds(j * GW, GW)] for h in range(2)]

    w2 = {n: a[n].rearrange("o k n -> (o k) n") for n in (
        "w_in", "w_attn_proj", "w_conv_proj", "w_out", "w_ffn_in", "w_ffn_out", "w_ada",
        "w_in_2", "w_up_a_2", "w_up_b_2", "w_out_2", "w_cq_2", "w_ckv_2", "w_co_2", "w_gate_up_2", "w_down_2")}

    STEPS = [(h, t) for h in range(HEADS) for t in range(TT)]

    block = nc.Block()
    ctx = ExitStack()
    ctx.enter_context(block)

    @block.sync
    def _(sp):
        sp.dma_start(mem_rows[:], a["mem_2"].rearrange("o (t p) d -> p (o t) d", p=P)).then_inc(sem["mem_landed"], 16)
        sp.dma_start(const[:], const_dram[:]).then_inc(sem["const_landed"], 16)
        rows = [("c", V_C, 8), ("norm_mix_g", V_MIX, 8), ("norm_ffn_g", V_FFN, 8), ("norm_mix_g_2", V_MIX2, 8),
                ("norm_cross_g_2", V_CROSS, 8), ("norm_mem_g_2", V_MEM, 8), ("norm_ffn_g_2", V_FFN2, 8),
                ("conv_ln_g", V_CLG, 4), ("conv_ln_b", V_CLB, 4), ("b_dw", V_BDW, 4), ("subln_g_2", V_SUB, 1),
                ("b_ada", V_ADA, 48)]
        for name, r, n in rows:
            sp.dma_start(vec_rows[r:r + n, :], a[name].rearrange("o (k p) -> (o k) p", p=P)).then_inc(small_landed, 16)
        sp.dma_start(tap_rows[:], a["w_dw"].rearrange("o t i c -> (o t i) c")).then_inc(small_landed, 16)

        def load(b, src, wide=None, i=0, step=0):
            if b >= RAW:
                sp.wait_ge(lo_ready, last_piece_of(b - RAW) + 1 + i * step)
            dst = raw[:, b % RAW, :]
            if wide == "small":
                dst = dst[:, 0:KD * SMALL].rearrange("p (k n) -> p k n", k=KD)
            elif wide == "pair":
                dst = dst.rearrange("p (k h n) -> p k h n", k=4, h=2)
                sp.dma_start(dst[:, :, 1, :], src[1]).then_inc(second_landed[b % RAW], 16)
                dst, src = dst[:, :, 0, :], src[0]
            elif wide == "long":
                dst = dst.rearrange("p (k n) -> p k n", k=2)
                if pair_blocks(b):
                    sp.dma_start(dst[:, 1, :], src[:, 1, :]).then_inc(second_landed[b % RAW], 16)
                    dst, src = dst[:, 0, :], src[:, 0, :]
            else:
                dst = dst.rearrange("p (k n) -> p k n", k=4)
            sp.dma_start(dst, src).then_inc(raw_landed[b % RAW], 16)

        for s in range(4):
            for k in range(2):
                load(2 * s + k, slab_src(w2["w_ckv_2"], 4 * k, s * W))
            if s == 0:
                sp.dma_start(x[:], a["x"].rearrange("o (t p) d -> p (o t) d", p=P)).then_inc(sem["x_landed"], 16)
        load(8, w2["w_in"].rearrange("(k p) n -> p k n", p=P)[:, :, C_KI:C_U], "small")
        for j in range(4):
            load(9 + j, slab_src(w2["w_in"], 4 * (j % 2), C_U + (j // 2) * W))
        with sp.Fori(0, 2) as i:
            for j in range(4):
                load(13 + j, slab_src(w2["w_in"], 4 * (j % 2), i * (2 * W) + (j // 2) * W), None, i, 8)
        with sp.Fori(0, 2) as i:
            for j in range(4):
                load(21 + j, slab_src(w2["w_in"], 4 * (j % 2), i * (2 * W) + (C_GA + (j // 2) * W)), None, i, 8)
        sp.dma_start(final_g[:], a["norm_final_g"].partition_broadcast(P)).then_inc(final_landed, 16)
        for n, name in enumerate(("lam_q1_2", "lam_k1_2", "lam_q2_2", "lam_k2_2")):
            sp.dma_start(lam[:, n, :], a[name].rearrange("o d -> (o d)").partition_broadcast(P)).then_inc(late_landed, 16)
        b = 29
        for c in range(2):
            load(b + c, slab_src(w2["w_attn_proj"], 0, c * W))
        for c in range(2):
            load(b + 2 + c, slab_src(w2["w_conv_proj"], 0, c * W))
        b = 33
        for j in range(4):
            load(b + j, slab_src(w2["w_out"], 4 * (j % 2), (j // 2) * W))

        def load_ff(b, win, wout):
            for j in range(2):
                load(b + j, pair_src(win, 4 * j, 0), "pair")
            with sp.Fori(0, 5) as i:
                for j in range(4):
                    load(b + 2 + j, pair_src(win, 4 * (j % 2), i * 2 + (1 + j // 2)), "pair", i, 8)
            b += 22
            v = wout.rearrange("(k p) n -> p k n", p=P)
            for j in range(3):
                load(b + j, v[:, 2 * j:2 * j + 2, :], "long")
            with sp.Fori(0, 2) as i:
                for j in range(4):
                    load(b + 3 + j, v[:, bass.ds(i * 8 + (6 + 2 * j), 2), :], "long", i, 8)

        load_ff(37, w2["w_ffn_in"], w2["w_ffn_out"])
        rb = a["rel_bias_2"].rearrange("o h r -> (o h) r")
        sp.wait_ge(sem["conv_lo"], 1)
        src = bass.AP(tensor=rb.tensor, offset=rb.offset + 1 + P, ap=[[1, P], [2 * SEQ + 1, HEADS], [1, SEQ]])
        sp.dma_start(rel_rows[:], src).then_inc(sem["rel_landed"], 16)
        with sp.Fori(0, 5) as i:
            for j in range(4):
                load(70 + j, slab_src(w2["w_in_2"], 4 * (j % 2), i * (2 * W) + (j // 2) * W), None, i, 8)
        for n, name in ((90, "w_up_b_2"), (92, "w_up_a_2")):
            for c in range(2):
                load(n + c, slab_src(w2[name], 0, c * W))
        for n, name in ((94, "w_out_2"), (98, "w_cq_2"), (102, "w_co_2")):
            for j in range(4):
                load(n + j, slab_src(w2[name], 4 * (j % 2), (j // 2) * W))
            if n == 94:
                sp.wait_ge(sem["final1_done"], TT)
                sp.dma_start(final_g[:], a["norm_final_g_2"].partition_broadcast(P)).then_inc(final_landed, 16)
        load_ff(106, w2["w_gate_up_2"], w2["w_down_2"])
        for t in range(TT):
            sp.wait_ge(sem["result"], t + 1)
            sp.dma_start(out.rearrange("o (t p) d -> p (o t) d", p=P)[:, t, :], x[:, t, :]).then_inc(out_done, 16)
        sp.wait_ge(out_done, 16 * TT)

    @block.gpsimd
    def _(pool):
        for m, g in ((2, g_mix), (5, g_ffn)):
            pool.dma_start(g[:], a["b_ada"].rearrange("o n -> (o n)")[m * D:(m + 1) * D].partition_broadcast(P))\
                .then_inc(sem["gate_bias_landed"], 16)

        def ada_block(n, s, k, i=0, step=0, wait=True):
            if wait:
                pool.wait_ge(ada_step, 4 * (n - 1) + i * (4 * step))
            pool.dma_start(ada_raw[:, n % 2, :].rearrange("p (k n) -> p k n", k=4),
                           slab_src(w2["w_ada"], 4 * k, s)).then_inc(ada_landed[n % 2], 16)

        def rstd(n):
            pool.wait_ge(nt["mean"], n + 1)
            pool.tensor_tensor(stat[:, 4:6], stat[:, 2:4], C("half", 0, 2), ALU.pow).then_inc(nt["rstd"], 1)

        for k in range(2):
            ada_block(k, 0, k, wait=False)
        pool.wait_ge(sem["const_landed"], 16)
        rstd(N_MEM)
        for n in range(2, 8):
            if n == 4:
                rstd(N_H1)
            ada_block(n, (n // 2) * W, n % 2)
        with pool.Fori(0, 6) as i:
            for k in range(2):
                ada_block(8 + k, i * W + 4 * W, k, i, 2)
        pool.wait_ge(sem["ln_var"], 1)
        pool.tensor_tensor(stat[:, 62:64], stat[:, 60:62], C("half", 0, TT), ALU.pow).then_inc(sem["ln_rstd"], 1)
        rstd(N_H2)
        pool.wait_ge(nt["lo"], 4 * F_OF[N_H2] + 4)
        for n in range(20, 24):
            ada_block(n, (n // 2) * W, n % 2)
        rstd(N_FINAL1)
        rstd(N_M2)
        pool.wait_ge(sem["sub_mean"], 1)
        pool.tensor_tensor(stat[:, 24:32], stat[:, 16:24], C("half", 0, 8), ALU.pow).then_inc(sem["sub_rstd"], 1)
        rstd(N_CR)
        rstd(N_F2)
        rstd(N_FINAL2)

    @block.tensor
    def _(pe):
        def mm3(ps, kt, t, hi, lo, wh, wl, start, stop):
            ts = slice(t * P, (t + 1) * P)
            pe.matmul(ps, hi[:, kt, ts], wh, start=start, stop=False)
            pe.matmul(ps, hi[:, kt, ts], wl, start=False, stop=False)
            return pe.matmul(ps, lo[:, kt, ts], wh, start=False, stop=stop)

        def piece(p, u, j, n, i=0, kbase=0, norm=None, ready=None, hidden=None, pair=None):
            pe.wait_ge(lo_ready, p + 1 + i * 8)
            if norm is not None:
                pe.wait_ge(nt["lo"], 4 * F_OF[norm] + j + 1)
            if ready is not None:
                pe.wait_ge(*ready)
            if j == 0 and u >= 2 and hidden is None:
                for t in range(TT):
                    pe.wait_ge(acc_free[t], u - (pair is None) + i * 2)
            elif j == 0 and hidden is not None:
                pe.wait_ge(hidden[0], hidden[1] + i * 4)
            wh = w_hi[:, p % RING, :].rearrange("p (k n) -> p k n", k=2)
            wl = w_lo[:, p % RING, :].rearrange("p (k n) -> p k n", k=2)
            for kk in range(2):
                kt = 2 * j + kk
                for t in range(TT):
                    last = mm3(bank[2 * (u % 2 if pair is None else pair) + t][:], kbase + kt, t, a_hi, a_lo,
                               wh[:, kk, :], wl[:, kk, :],
                               kt == 0, kt == 2 * n - 1)
            last.then_inc(piece_used, 1)

        def slab(p, u, i=0, norm=None):
            for j in range(4):
                piece(p + j, u, j, 4, i, 0, norm)

        def turn(n, src):
            for g in range(4):
                if g == 0:
                    pe.wait_ge(nt["rows0"], F_OF[n] + 1)
                    pe.wait_ge(nt["rows1"], F_OF[n] + 1)
                for kk in range(2):
                    kt = 2 * g + kk
                    for t in range(TT):
                        last = pe.transpose(bank[4 + g][:, kk * SEQ + t * P:kk * SEQ + (t + 1) * P],
                                            src[:, t, kt * P:(kt + 1) * P], ident)
                last.then_inc(nt["turned"], 1)

        def turn_x(ready):
            for t in range(TT):
                pe.wait_ge(*ready(t))
                for kt in range(KD):
                    last = pe.transpose(bank[4 + kt // 2][:, (kt % 2) * SEQ + t * P:(kt % 2) * SEQ + (t + 1) * P],
                                        x[:, t, kt * P:(kt + 1) * P], ident)
                    if t == TT - 1 and kt % 2:
                        last.then_inc(nt["turned"], 1)

        def turn4(b0, src_cols, src, done, n=CG):
            for g in range((n + 1) // 2):
                for kk in range(min(2, n - 2 * g)):
                    c = src_cols + (2 * g + kk) * P
                    for t in range(TT):
                        last = pe.transpose(bank[b0 + g][:, kk * SEQ + t * P:kk * SEQ + (t + 1) * P],
                                            src[:, t, c:c + P], ident)
                last.then_inc(done, 1)

        pe.wait_ge(sem["const_landed"], 16)
        pe.wait_ge(small_landed, 16 * 13)
        pe.transpose(bank[7][:, 0:V_ROWS], vec_rows[0:V_ROWS, :], ident[0:V_ROWS, 0:V_ROWS])
        for g in range(CG):
            last = pe.transpose(bank[7][:, P + g * TAPS:P + (g + 1) * TAPS], tap_rows[:, g * P:(g + 1) * P],
                                ident[0:TAPS, 0:TAPS])
        last.then_inc(sem["vec_turned"], 1)
        pe.wait_ge(sem["vec_copied"], 2)
        turn(N_MEM, xs_z)
        for s in range(4):
            slab(P_CKV + 4 * s, U_CKV + s, norm=N_MEM if s == 0 else None)
            if s == 2:
                pe.wait_ge(acc_free[0], 2)
                pe.wait_ge(acc_free[1], 2)
                for g in range(4):
                    for kk in range(2):
                        kt = 2 * g + kk
                        for t in range(TT):
                            last = pe.transpose(bank[4 + g][:, kk * SEQ + t * P:kk * SEQ + (t + 1) * P],
                                                k_rows[:, t, kt * P:(kt + 1) * P], ident)
                    last.then_inc(sem["key_turned"], 1)
        pe.wait_ge(ada_step, 8 * 4)
        pe.wait_ge(sem["key_copied"], 4)
        for j in range(16):
            last = pe.matmul(bank[4][:, j:j + 1], ada_acc[:, j // 4, (j % 4) * P:(j % 4 + 1) * P], ones[:, 0:1],
                             start=True, stop=True)
        last.then_inc(sem["ada_reduced"], 1)
        pe.wait_ge(sem["mod_copied"], 1)
        turn(N_H1, xs_z)
        pe.wait_ge(lo_ready, P_SMALL + 1)
        for t in range(TT):
            pe.wait_ge(acc_free[t], U_SMALL - 1)
        pe.wait_ge(nt["lo"], 4 * N_H1 + 4)
        sm_hi = w_hi[:, P_SMALL % RING, 0:KD * SMALL].rearrange("p (k n) -> p k n", k=KD)
        sm_lo = w_lo[:, P_SMALL % RING, 0:KD * SMALL].rearrange("p (k n) -> p k n", k=KD)
        for t in range(TT):
            for kt in range(KD):
                last = mm3(bank[2 * (U_SMALL % 2) + t][:, 0:SMALL], kt, t, a_hi, a_lo, sm_hi[:, kt, :],
                           sm_lo[:, kt, :], kt == 0, kt == KD - 1)
        last.then_inc(piece_used, 1)
        for s in range(2):
            slab(P_IN1 + 4 * s, U_IN1 + s)
        with pe.Fori(0, 2) as i:
            for s in range(2):
                slab(P_IN1 + 8 + 4 * s, U_IN1 + 2 + s, i)

        def reduce_gate(step, slot):
            pe.wait_ge(ada_step, step)
            for c in range(2):
                last = pe.matmul(bank[6 + c][:], ones, ada_acc[:, slot + c, :], start=True, stop=True)
            return last

        pe.wait_ge(acc_free[0], U_IN1 + 6)
        pe.wait_ge(acc_free[1], U_IN1 + 6)
        turn4(4, C_QI, z, sem["t1"])
        pe.wait_ge(sem["ki_copied"], 1)
        for t in range(TT):
            last = pe.transpose(bank[2][:, t * P:(t + 1) * P], ki2[:, t, :, :].rearrange("p a d -> p (a d)"), ident)
        last.then_inc(sem["t1"], 1)
        turn4(0, C_Q, z, sem["t1"])
        pe.wait_ge(sem["glu"], TT)
        turn4(6, C_U, z, sem["conv_turned"])
        pe.wait_ge(sem["t1_copied_act"], 2)
        pe.wait_ge(sem["t1_copied_dve"], 1)
        for n, (t, h) in enumerate([(t, h) for t in range(TT) for h in range(HEADS)]):
            keys = P * (t + 1)
            if n >= 2:
                pe.wait_ge(sem["relu_done"], n - 1)
            half = slice(64 * (h % 2), 64 * (h % 2) + 64)
            pe.matmul(bank[4 + n % 2][:, 0:keys], qiT[half, h // 2, t * P:(t + 1) * P], kiT[half, 0:keys],
                      start=True, stop=True).then_inc(sem["logits"], 1)
        pe.wait_ge(sem["relu_done"], 16)
        turn4(4, C_K, z, sem["t1"])
        slab(P_IN1 + 24, U_IN1 + 6)
        pe.wait_ge(sem["t1_copied_act"], 4)
        pe.wait_ge(sem["t1_copied_dve"], 3)
        reduce_gate(8 * 10, 0)
        for j in range(16):
            last = pe.matmul(bank[4][:, j:j + 1], ada_acc[:, 2 + j // 4, (j % 4) * P:(j % 4 + 1) * P], ones[:, 0:1],
                             start=True, stop=True)
        last.then_inc(sem["ada_reduced"], 1)
        slab(P_IN1 + 28, U_IN1 + 7)

        def attention(tag, q, k, v_cols, pv_banks, between=None):
            def scores(n):
                h, t = STEPS[n]
                keys = P * (t + 1)
                half = slice(64 * (h % 2), 64 * (h % 2) + 64)
                if n >= 2:
                    pe.wait_ge(*after(tag, "max", n - 1))
                pe.matmul(bank[4 + n % 2][:, 0:keys], q[half, h // 2, t * P:(t + 1) * P], k[half, h // 2, 0:keys],
                          start=True, stop=True).then_inc(event(tag, "scores"), 1)

            def turn_p(n):
                h, t = STEPS[n]
                pe.wait_ge(*after(tag, "exp", n + 1))
                if n >= 1:
                    pe.wait_ge(*after(tag, "pT", n))
                for kt in range(t + 1):
                    last = pe.transpose(bank[6][:, kt * P:(kt + 1) * P], p_work[:, n % 2, 0, kt * P:(kt + 1) * P], ident)
                last.then_inc(event(tag, "turned"), 1)

            def values(n):
                h, t = STEPS[n]
                pe.wait_ge(*after(tag, "pT", n + 1))
                for kt in range(t + 1):
                    last = pe.matmul(bank[pv_banks + t][:, h * DH:(h + 1) * DH], pT[:, n % 2, kt, :],
                                     z[:, kt, v_cols + h * DH:v_cols + (h + 1) * DH],
                                     start=(kt == 0), stop=(kt == t))
                last.then_inc(event(tag, "pv"), 1)

            scores(0)
            scores(1)
            for n in range(len(STEPS)):
                turn_p(n)
                if n + 2 < len(STEPS):
                    scores(n + 2)
                if between is not None and n % 2:
                    between(n // 2)
                if n >= 1:
                    values(n - 1)
            values(len(STEPS) - 1)

        def second_gate(j):
            piece(P_IN1 + 32 + j, U_IN1 + 8 + j // 4, j % 4, 4, pair=1)

        for t in range(TT):
            pe.wait_ge(acc_free[t], U_IN1 + 8)
        pe.wait_ge(sem["mod_copied"], 2)
        attention("a1_", qT, kT, C_V, 0, second_gate)
        pe.wait_ge(sem["conv_done"], 4 * TAPS)
        pe.wait_ge(*after("a1_", "max", 16))
        for g in range(CG):
            last = pe.matmul(bank[4][:, 0:SEQ], mean512, conv_out[:, g, :], start=(g == 0), stop=(g == CG - 1))
        last.then_inc(sem["ln_mean"], 1)
        pe.wait_ge(sem["y1"], TT)
        turn4(6, 0, z, sem["y1_turned"])
        pe.wait_ge(sem["ln_square"], 1)
        for t in range(TT):
            for g in range(CG):
                last = pe.matmul(bank[5][:, t:t + 1], conv_sq[:, g, t * P:(t + 1) * P], mean512[:, 0:1],
                                 start=(g == 0), stop=(g == CG - 1))
        last.then_inc(sem["ln_sumsq"], 1)

        def half_columns(p, u, c, ready, kbase):
            for j in range(2):
                piece(p + 2 * c + j, u + c, j, 2, 0, kbase, None, ready)

        for t in range(TT):
            pe.wait_ge(acc_free[t], U_PA)
        pe.wait_ge(sem["ln_diagonal"], 1)
        pe.matmul(bank[4][:, 0:SEQ], ones, conv_sq[:, 0, :], start=True, stop=True).then_inc(sem["ln_spread"], 1)
        for c in range(2):
            half_columns(P_PA, U_PA, c, (sem["y1_lo"], 2), 0)
        for c in range(2):
            half_columns(P_PC, U_PC, c, (sem["conv_lo"], 1), 4)

        def turn_merged(tag):
            for g in range(4):
                if g % 2 == 0:
                    pe.wait_ge(*after(tag, "merged", TT * (g // 2 + 1)))
                for kk in range(2):
                    kt = 2 * g + kk
                    for t in range(TT):
                        last = pe.transpose(bank[4 + g][:, kk * SEQ + t * P:kk * SEQ + (t + 1) * P],
                                            z[:, t, kt * P:(kt + 1) * P], ident)
                last.then_inc(event(tag, "merged_turned"), 1)

        def project(p, u, tag):
            for s in range(2):
                for j in range(4):
                    piece(p + 4 * s + j, u + s, j, 4, 0, 0, None, after(tag, "lo", j + 1) if s == 0 else None)

        turn_merged("m1_")
        project(P_OUT1, U_OUT1, "m1_")
        turn(N_H2, xs_u)

        def feed_forward(p, u, norm, tag, gate_slot=None):
            def turn_hidden(s, wait, i=0):
                pe.wait_ge(*after(tag, "hidden", wait + i * 4))
                for kk in range(2):
                    for t in range(TT):
                        last = pe.transpose(bank[4 + s % 2][:, kk * SEQ + t * P:kk * SEQ + (t + 1) * P],
                                            ff_hid[:, t, kk * P:(kk + 1) * P], ident)
                last.then_inc(event(tag, "hidden_turned"), 1)

            slab(p, u, 0, norm)
            for t in range(TT):
                pe.wait_ge(acc_free[t], u)
            with pe.Fori(0, 5) as i:
                for s in (1, 2):
                    for j in range(4):
                        piece(p + 4 * s + j, u + s, j, 4, i, hidden=after(tag, "hidden", TT * (s - 1)))
                        if j == 1:
                            turn_hidden(s - 1, TT * s, i)
            p += 4 * NSLAB_FF
            pe.wait_ge(*after(tag, "hidden", TT * NSLAB_FF))
            for kt in range(KF):
                if kt == 2:
                    turn_hidden(NSLAB_FF - 1, TT * NSLAB_FF)
                if kt == KF - 2 and gate_slot is not None:
                    reduce_gate(8 * 12, gate_slot).then_inc(sem["ada_reduced"], 1)
                pe.wait_ge(lo_ready, p + kt + 1)
                pe.wait_ge(*after(tag, "hidden_lo", kt // 2 + 1))
                wh, wl = w_hi[:, (p + kt) % RING, :], w_lo[:, (p + kt) % RING, :]
                for t in range(TT):
                    ts = slice(t * P, (t + 1) * P)
                    for n, (lhs, w) in enumerate(((f_hi, wh), (f_hi, wl), (f_lo, wh))):
                        for c in range(2):
                            last = pe.matmul(bank[2 * t + c][:], lhs[:, kt, ts], w[:, c * W:(c + 1) * W],
                                             start=(kt == 0 and n == 0), stop=(kt == KF - 1 and n == 2))
                last.then_inc(piece_used, 1)

        feed_forward(P_FI1, U_FI1, N_H2, "f1_", 4)
        turn_x(lambda t: (sem["final1_done"], t + 1))
        pe.wait_ge(nt["lo"], 4 * F_OF[N_M2] + 4)
        with pe.Fori(0, 3) as i:
            for s in range(2):
                slab(P_IN2 + 4 * s, U_IN2 + s, i)

        pe.wait_ge(acc_free[0], U_IN2 + 6)
        pe.wait_ge(acc_free[1], U_IN2 + 6)
        turn4(4, E_QB, z, sem["t2"])
        turn4(6, E_KB, z, sem["t2"])
        pe.wait_ge(sem["rope_sum"], TT)
        turn4(0, E_QA, z, sem["t2"])
        turn4(2, E_KA, z, sem["t2"])
        pe.wait_ge(sem["t2_copied_act"], 4)
        pe.wait_ge(sem["t2_copied_dve"], 4)

        def gates(j):
            piece(P_IN2 + 24 + j, U_IN2 + 6 + j // 4, j % 4, 4, pair=1)

        attention("b_", qbT, kbT, E_VB, 0, gates)

        DS = [(h, t) for h in range(4) for t in range(TT)]

        def d_scores(n):
            h, t = DS[n]
            keys = P * (t + 1)
            for c in range(2):
                m = 2 * n + c
                if m >= len(D_BANKS):
                    pe.wait_ge(*after("d_", "max", m - len(D_BANKS) + 1))
                half = slice(64 * c, 64 * c + 64)
                last = pe.matmul(bank[D_BANKS[m % len(D_BANKS)]][:, 0:keys], qaT[half, h, t * P:(t + 1) * P],
                                 kaT[half, h, 0:keys], start=True, stop=True)
            last.then_inc(event("d_", "scores"), 1)

        def d_turn(n):
            h, t = DS[n]
            pe.wait_ge(*after("d_", "mix", n + 1))
            if n >= 1:
                pe.wait_ge(*after("d_", "pT", n))
            for kt in range(t + 1):
                last = pe.transpose(bank[6][:, kt * P:(kt + 1) * P], p_work[:, n % 2, 0, kt * P:(kt + 1) * P], ident)
            last.then_inc(event("d_", "turned"), 1)

        def d_values(n):
            h, t = DS[n]
            pe.wait_ge(*after("d_", "pT", n + 1))
            for kt in range(t + 1):
                last = pe.matmul(bank[t][:, h * P:(h + 1) * P], pT[:, n % 2, kt, :],
                                 z[:, kt, E_VA + h * P:E_VA + (h + 1) * P], start=(kt == 0), stop=(kt == t))
            last.then_inc(event("d_", "pv"), 1)

        pe.wait_ge(*after("b_", "max", 16))
        pe.wait_ge(*after("b_", "pT", 16))
        d_scores(0)
        d_scores(1)
        for n in range(len(DS)):
            d_turn(n)
            if n + 2 < len(DS):
                d_scores(n + 2)
            gates(8 + n)
            if n == 1:
                pe.wait_ge(sem["yb"], TT)
            if n >= 1:
                d_values(n - 1)
        d_values(len(DS) - 1)
        pe.wait_ge(*after("d_", "pT", 8))
        turn4(6, W, z, sem["y2_turned"])
        for t in range(TT):
            pe.wait_ge(acc_free[t], U_UB)
        half_columns(P_UB, U_UB, 0, (sem["y2_lo"], 2), 4)
        pe.wait_ge(sem["ya"], TT)
        turn4(4, 0, z, sem["y2_turned"])
        half_columns(P_UB, U_UB, 1, (sem["y2_lo"], 2), 4)
        for c in range(2):
            half_columns(P_UA, U_UA, c, (sem["y2_lo"], 4), 0)
        turn_merged("m2_")
        project(P_OUT2, U_OUT2, "m2_")

        turn_x(updated(U_OUT2 + 2))
        for s in range(2):
            slab(P_CQ + 4 * s, U_CQ + s, 0, (N_CR) if s == 0 else None)
        pe.wait_ge(acc_free[0], U_CQ + 2)
        pe.wait_ge(acc_free[1], U_CQ + 2)
        for g in range(4):
            for kk in range(2):
                kt = 2 * g + kk
                for t in range(TT):
                    last = pe.transpose(bank[4 + g][:, kk * SEQ + t * P:kk * SEQ + (t + 1) * P],
                                        qx_rows[:, t, kt * P:(kt + 1) * P], ident)
            last.then_inc(sem["qx_turned"], 1)

        def x_scores(n):
            h, t = DS[n]
            if n >= 2:
                pe.wait_ge(*after("x_", "exp", n - 1))
            for kk in range(2):
                last = pe.matmul(bank[4 + n % 2][:, 0:SEQ], qxT[:, 2 * h + kk, t * P:(t + 1) * P],
                                 mem_kT[:, 2 * h + kk, :], start=(kk == 0), stop=(kk == 1))
            last.then_inc(event("x_", "scores"), 1)

        def x_turn(n):
            pe.wait_ge(*after("x_", "exp", n + 1))
            if n >= 1:
                pe.wait_ge(*after("x_", "pT", n))
            for kt in range(TT):
                last = pe.transpose(bank[6][:, kt * P:(kt + 1) * P], p_work[:, n % 2, 0, kt * P:(kt + 1) * P], ident)
            last.then_inc(event("x_", "turned"), 1)

        def x_values(n):
            h, t = DS[n]
            pe.wait_ge(*after("x_", "pT", n + 1))
            for kt in range(TT):
                last = pe.matmul(bank[2 * (h // 2) + t][:, (h % 2) * SEQ:(h % 2 + 1) * SEQ], pT[:, n % 2, kt, :],
                                 mem_v[:, kt, h * SEQ:(h + 1) * SEQ], start=(kt == 0), stop=(kt == TT - 1))
            last.then_inc(event("x_", "pv"), 1)

        pe.wait_ge(sem["qx_copied_act"], 2)
        pe.wait_ge(sem["qx_copied_dve"], 2)
        x_scores(0)
        for n in range(len(DS)):
            if n + 1 < len(DS):
                x_scores(n + 1)
            x_turn(n)
            if n >= 1:
                x_values(n - 1)
        x_values(len(DS) - 1)
        pe.wait_ge(*after("x_", "pT", 8))
        turn_merged("m3_")
        project(P_CO, U_CO, "m3_")
        turn_x(updated(U_CO + 2))
        feed_forward(P_FI2, U_FI2, N_F2, "f2_")

    @block.scalar
    def _(act):
        def conv(p, n=1, i=0):
            for q in range(p, p + n):
                b, half = block_of(q)
                act.wait_ge(raw_landed[b % RAW], 16 * (b // RAW + 1) + i * 16)
                if pair_blocks(b):
                    act.wait_ge(second_landed[b % RAW], 16 * pair_blocks(b) + i * 16)
                if q >= RING:
                    act.wait_ge(piece_used, q - RING + 1 + i * 8)
                m = KD * SMALL if q == P_SMALL else PIECE
                act.activation(w_hi[:, q % RING, 0:m], raw[:, b % RAW, half * PIECE:half * PIECE + m], ACT.Copy)\
                    .then_inc(hi_ready, 1)

        def two(b):
            return bank[b][:].rearrange("p (k n) -> p k n", k=2)

        def sumsq(n, src, junk, done=None):
            for t in range(TT):
                if done is not None:
                    act.wait_ge(*done(t))
                act.activation(junk[:, t, :], src[:, t, :], ACT.Square, accum_out=stat[:, t:t + 1])\
                    .then_inc(nt["sumsq"], 1)

        def rows1(n, src, dst):
            act.wait_ge(nt["rstd"], n + 1)
            act.wait_ge(nt["sumsq"], TT * (n + 1))
            act.activation(dst[:, 1, :], src[:, 1, :], ACT.Copy, scale=stat[:, 5:6]).then_inc(nt["rows1"], 1)

        def features(n, f, gain, shift, between=None):
            fi = F_OF[n]
            for g in (0, 2):
                act.wait_ge(nt["turned"], 4 * fi + g + 1)
                for kk in range(2):
                    kt = 2 * g + kk
                    last = act.activation(f[:, kt, :], bank[4 + g][:, kk * SEQ:(kk + 1) * SEQ], ACT.Identity,
                                          scale=gain[:, kt:kt + 1],
                                          bias=0.0 if shift is None else shift[:, kt:kt + 1])
                last.then_inc(nt["feat_act"], 1)
            for g in range(4):
                act.wait_ge(nt["feat_dve" if g % 2 else "feat_act"], 2 * fi + g // 2 + 1)
                act.activation(a_hi[:, 2 * g:2 * g + 2, :], f[:, 2 * g:2 * g + 2, :], ACT.Copy).then_inc(nt["hi"], 1)
                if between is not None:
                    conv(between + g)

        def features_x(n, gain):
            fi = F_OF[n]
            for g in range(4):
                act.wait_ge(nt["turned"], 4 * fi + g + 1)
                for kk in range(2):
                    kt = 2 * g + kk
                    last = act.activation(a_hi[:, kt, :], bank[4 + g][:, kk * SEQ:(kk + 1) * SEQ], ACT.Copy,
                                          scale=gain[:, kt:kt + 1])
                last.then_inc(nt["hi"], 1)

        def copy_pair(done, n, dst, b, copied):
            act.wait_ge(done, n)
            act.activation(dst, two(b), ACT.Copy).then_inc(copied, 1)

        act.wait_ge(sem["mem_landed"], 16)
        sumsq(N_MEM, mem_rows, xs_z)
        rows1(N_MEM, mem_rows, xs_z)
        act.wait_ge(sem["vec_copied"], 1)
        act.activation(stat[:, 8:16], vt[:, V_C:V_C + 8], ACT.Silu).then_inc(sem["c_act"], 1)
        features(N_MEM, f_z, vt[:, V_MEM:V_MEM + 8], None, P_CKV)
        for s in range(4):
            if s < 3:
                conv(P_CKV + 4 * s + 4, 4)
            else:
                conv(P_SMALL)
            act.wait_ge(piece_used, P_CKV + 4 * s + 4)
            dst = k_rows if s < 2 else mem_v
            act.activation(dst[:, 0, (s % 2) * W:(s % 2 + 1) * W], bank[2 * (s % 2)][:], ACT.Copy)\
                .then_inc(acc_free[0], 1)
            if s == 2:
                for g in (0, 2):
                    copy_pair(sem["key_turned"], g + 1, mem_kT[:, 2 * g:2 * g + 2, :], 4 + g, sem["key_copied"])
            if s == 0:
                act.wait_ge(sem["x_landed"], 16)
                sumsq(N_H1, x, xs_z)
                rows1(N_H1, x, xs_z)
        act.wait_ge(sem["gains"], 1)
        features(N_H1, f_z, gain1, modT[:, 0:8])
        conv(P_IN1, 4)
        act.wait_ge(piece_used, P_SMALL + 1)
        for t in range(TT):
            act.activation(z[:, t, C_KI:C_U], bank[2 * (U_SMALL % 2) + t][:, 0:SMALL], ACT.Copy)\
                .then_inc(acc_free[t], 1)

        def slab_out(p, u, c, func, i=0, pair=None, scaled=False):
            act.wait_ge(piece_used, p + 1 + i * 8)
            for t in range(TT):
                act.activation(z[:, t, bass.ds(i * (2 * W) + c, W)] if not isinstance(i, int) else z[:, t, c:c + W],
                               bank[2 * (u % 2 if pair is None else pair) + t][:], func,
                               scale=stat[:, 4 + t:5 + t] if scaled else 1.0).then_inc(acc_free[t], 1)

        def project_slabs(p, u, c0, n):
            with act.Fori(0, n // 2) as i:
                for s in range(2):
                    conv(p + 4 * s + 4, 4, i)
                    act.wait_ge(piece_used, p + 4 * s + 4 + i * 8)
                    act.activation(z[:, 0, bass.ds(i * (2 * W) + (c0 + s * W), W)], bank[2 * ((u + s) % 2)][:],
                                   ACT.Copy, scale=stat[:, 4:5]).then_inc(acc_free[0], 1)

        for s in range(2):
            conv(P_IN1 + 4 * s + 4, 4)
            slab_out(P_IN1 + 4 * s + 3, U_IN1 + s, C_U + s * W, ACT.Sigmoid if s else ACT.Copy)
        with act.Fori(0, 2) as i:
            for s in range(2):
                conv(P_IN1 + 8 + 4 * s + 4, 4, i)
                slab_out(P_IN1 + 8 + 4 * s + 3, U_IN1 + 2 + s, s * W, ACT.Copy, i)

        act.wait_ge(ada_step, 8 * 10)
        copy_pair(sem["t1"], 1, qiT[:, 0:2, :], 4, sem["t1_copied_act"])
        act.wait_ge(sem["t1"], 3)
        act.activation(kiT[:], bank[2][:, 0:SEQ], ACT.Copy).then_inc(sem["t1_copied_act"], 1)
        copy_pair(sem["t1"], 4, qT[:, 0:2, :], 0, sem["t1_copied_act"])
        act.wait_ge(sem["conv_turned"], 1)
        act.wait_ge(sem["pad_zeroed"], 1)
        act.activation(conv_in[:, 0:2, PAD:], two(6), ACT.Copy).then_inc(sem["conv_in_act"], 1)
        for n in range(TT * HEADS):
            keys = P * (n // HEADS + 1)
            act.wait_ge(sem["logits"], n + 1)
            if n >= 2:
                act.wait_ge(sem["score_step"], n - 1)
            act.activation(relu_t[:, n % 2, 0:keys], bank[4 + n % 2][:, 0:keys], ACT.Relu, scale=DH ** -0.5)\
                .then_inc(sem["relu_done"], 1)
        copy_pair(sem["t1"], 6, kT[:, 0:2, :], 4, sem["t1_copied_act"])
        for s in range(2):
            conv(P_IN1 + 28 + 4 * s, 4)
            slab_out(P_IN1 + 27 + 4 * s, U_IN1 + 6 + s, C_GA + s * W, ACT.Sigmoid)

        def softmax_steps(tag, between=None):
            for n, (h, t) in enumerate(STEPS):
                keys = P * (t + 1)
                act.wait_ge(*after(tag, "negmax", n + 1))
                if n >= 2:
                    act.wait_ge(*after(tag, "turned", n - 1))
                act.activation(p_work[:, n % 2, 0, 0:keys], s_work[:, n % 2, 0, 0:keys], ACT.Exp,
                               bias=stat[:, 34 + n % 2:35 + n % 2], accum_out=stat[:, 36 + t * 8 + h:37 + t * 8 + h])\
                    .then_inc(event(tag, "exp"), 1)
                if between is not None:
                    between(n)
                act.wait_ge(*after(tag, "turned", n + 1))
                if n >= 2:
                    act.wait_ge(*after(tag, "pv", n - 1))
                act.activation(pT[:, n % 2, 0:t + 1, :], bank[6][:, 0:keys].rearrange("p (k n) -> p k n", k=t + 1),
                               ACT.Copy).then_inc(event(tag, "pT"), 1)

        def second_gate(n):
            if n >= 4 and n % 2 == 0:
                conv(P_IN1 + 36 + (n - 4) // 2)
            if n == 8:
                slab_out(P_IN1 + 35, U_IN1 + 8, C_GB, ACT.Sigmoid, pair=1)

        softmax_steps("a1_", second_gate)
        conv(P_IN1 + 42, 2)
        slab_out(P_IN1 + 39, U_IN1 + 9, C_GB + W, ACT.Sigmoid, pair=1)
        for g in range(2):
            act.wait_ge(sem["y1_turned"], g + 1)
            act.activation(a_hi[:, 2 * g:2 * g + 2, :], two(6 + g), ACT.Copy).then_inc(sem["y1_hi"], 1)
        act.wait_ge(sem["ln_scaled"], 1)
        for g in range(CG):
            last = act.activation(conv_in[:, g, 0:SEQ], conv_out[:, g, :], ACT.Silu,
                                  scale=vt[:, V_CLG + g:V_CLG + g + 1], bias=vt[:, V_CLB + g:V_CLB + g + 1])
        last.then_inc(sem["swish"], 1)
        act.wait_ge(sem["swish"], 1)
        act.activation(a_hi[:, 4:8, :], conv_in[:, :, 0:SEQ], ACT.Copy).then_inc(sem["conv_hi"], 1)
        conv(P_PC, 4)
        conv(P_OUT1, 4)

        def merged_hi(tag):
            for g in range(4):
                act.wait_ge(*after(tag, "merged_turned", g + 1))
                act.activation(a_hi[:, 2 * g:2 * g + 2, :], two(4 + g), ACT.Copy).then_inc(event(tag, "hi"), 1)

        merged_hi("m1_")
        conv(P_OUT1 + 4, 4)
        conv(P_FI1, 4)
        sumsq(N_H2, x, xs_u, updated(U_OUT1 + 2))
        rows1(N_H2, x, xs_u)
        features(N_H2, f_u, gain2, modT[:, 24:32])

        def feed_forward(p, u, tag, following, scaled=False):
            def silu(s, i=0):
                act.wait_ge(piece_used, p + 4 * s + 4 + i * 8)
                for t in range(TT):
                    act.activation(ff_act[:, t, :], bank[2 * ((u + s) % 2) + t][:, 0:GW], ACT.Silu,
                                   scale=stat[:, 4 + t:5 + t] if scaled else 1.0)\
                        .then_inc(event(tag, "silu"), 1)

            def hidden_hi(s, dst, i=0):
                act.wait_ge(*after(tag, "hidden_turned", s + 1 + i * 2))
                act.activation(dst, two(4 + s % 2), ACT.Copy).then_inc(event(tag, "hidden_hi"), 1)

            conv(p + 4, 4)
            with act.Fori(0, 5) as i:
                for s in (1, 2):
                    silu(s - 1, i)
                    conv(p + 4 * s + 4, 2, i)
                    hidden_hi(s - 1, f_hi[:, bass.ds(i * 4 + (2 * s - 2), 2), :], i)
                    conv(p + 4 * s + 6, 2, i)
            last = NSLAB_FF - 1
            silu(last)
            p += 4 * NSLAB_FF
            conv(p + 4, 2)
            hidden_hi(last, f_hi[:, 2 * last:2 * last + 2, :])
            with act.Fori(0, 2) as i:
                conv(p + 6, 8, i)
            conv(p + KF, following)

        feed_forward(P_FI1, U_FI1, "f1_", 4)
        sumsq(N_FINAL1, x, xs_u, updated(U_FI1 + 2))
        features_x(N_M2, vt[:, V_MIX2:V_MIX2 + 8])
        sumsq(N_M2, x, xs_u, lambda t: (sem["final1_done"], t + 1))
        act.wait_ge(nt["rstd"], N_M2 + 1)
        project_slabs(P_IN2, U_IN2, 0, 6)

        copy_pair(sem["t2"], 1, qbT[:, 0:2, :], 4, sem["t2_copied_act"])
        copy_pair(sem["t2"], 3, kbT[:, 0:2, :], 6, sem["t2_copied_act"])
        act.wait_ge(sem["lam_dots"], 2)
        act.activation(stat[:, 56:58], stat[:, 54:56], ACT.Exp).then_inc(sem["lam_exp"], 1)
        copy_pair(sem["t2"], 5, qaT[:, 0:2, :], 0, sem["t2_copied_act"])
        copy_pair(sem["t2"], 7, kaT[:, 0:2, :], 2, sem["t2_copied_act"])

        def gates(n):
            if n >= 4 and n % 2 == 0:
                conv(P_IN2 + 28 + (n - 4) // 2)
            if n == 8:
                slab_out(P_IN2 + 27, U_IN2 + 6, E_GA, ACT.Sigmoid, pair=1, scaled=True)

        softmax_steps("b_", gates)
        conv(P_IN2 + 34, 2)
        slab_out(P_IN2 + 31, U_IN2 + 7, E_GA + W, ACT.Sigmoid, pair=1, scaled=True)
        for n in range(8):
            keys = P * (n % 2 + 1)
            act.wait_ge(*after("d_", "negmax", n + 1))
            if n >= 2:
                act.wait_ge(*after("d_", "turned", n - 1))
            for c in range(2):
                k = 2 * (n % 2) + c
                act.activation(p_work[:, n % 2, c, 0:keys], s_work[:, n % 2, c, 0:keys], ACT.Exp,
                               bias=d_stat[:, 4 + k:5 + k], accum_out=d_stat[:, 8 + k:9 + k]).then_inc(event("d_", "exp"), 1)
            if n >= 2:
                conv(P_IN2 + 34 + n)
            if n == 5:
                slab_out(P_IN2 + 35, U_IN2 + 8, E_GB, ACT.Sigmoid, pair=1, scaled=True)
            act.wait_ge(*after("d_", "turned", n + 1))
            if n >= 2:
                act.wait_ge(*after("d_", "pv", n - 1))
            act.activation(pT[:, n % 2, 0:n % 2 + 1, :], bank[6][:, 0:keys].rearrange("p (k n) -> p k n", k=n % 2 + 1),
                           ACT.Copy).then_inc(event("d_", "pT"), 1)
        conv(P_IN2 + 42, 2)
        slab_out(P_IN2 + 39, U_IN2 + 9, E_GB + W, ACT.Sigmoid, pair=1, scaled=True)
        for g in range(2):
            act.wait_ge(sem["y2_turned"], 1 + g)
            act.activation(a_hi[:, 4 + 2 * g:6 + 2 * g, :], two(6 + g), ACT.Copy).then_inc(sem["y2_hi"], 1)
        for g in range(2):
            act.wait_ge(sem["ya_feat"], g + 1)
            act.activation(a_hi[:, 2 * g:2 * g + 2, :], f_u[:, 2 * g:2 * g + 2, :], ACT.Copy).then_inc(sem["y2_hi"], 1)
        conv(P_UA, 4)
        conv(P_OUT2, 4)
        merged_hi("m2_")
        conv(P_OUT2 + 4, 4)
        conv(P_CQ, 4)
        features_x(N_CR, vt[:, V_CROSS:V_CROSS + 8])
        sumsq(N_CR, x, xs_u, updated(U_OUT2 + 2))
        act.wait_ge(nt["rstd"], N_CR + 1)
        for s in range(2):
            conv(P_CQ + 4 + 4 * s, 4)
            act.wait_ge(piece_used, P_CQ + 4 * s + 4)
            act.activation(qx_rows[:, 0, s * W:(s + 1) * W], bank[2 * ((U_CQ + s) % 2)][:], ACT.Copy,
                           scale=stat[:, 4:5])\
                .then_inc(acc_free[0], 1)
        for g in (0, 2):
            copy_pair(sem["qx_turned"], g + 1, qxT[:, 2 * g:2 * g + 2, :], 4 + g, sem["qx_copied_act"])
        for n in range(8):
            h, t = n // 2, n % 2
            act.wait_ge(*after("x_", "negmax", n + 1))
            if n >= 2:
                act.wait_ge(*after("x_", "turned", n - 1))
            act.activation(p_work[:, n % 2, 0, :], bank[4 + n % 2][:, 0:SEQ], ACT.Exp, scale=1.0 / 16,
                           bias=stat[:, 34 + n % 2:35 + n % 2], accum_out=stat[:, 36 + t * 4 + h:37 + t * 4 + h])\
                .then_inc(event("x_", "exp"), 1)
            act.wait_ge(*after("x_", "turned", n + 1))
            if n >= 2:
                act.wait_ge(*after("x_", "pv", n - 1))
            act.activation(pT[:, n % 2, :, :], bank[6][:, 0:SEQ].rearrange("p (k n) -> p k n", k=2), ACT.Copy)\
                .then_inc(event("x_", "pT"), 1)
        merged_hi("m3_")
        conv(P_CO + 4, 4)
        conv(P_FI2, 4)
        features_x(N_F2, vt[:, V_FFN2:V_FFN2 + 8])
        sumsq(N_F2, x, xs_u, updated(U_CO + 2))
        act.wait_ge(nt["rstd"], N_F2 + 1)
        feed_forward(P_FI2, U_FI2, "f2_", 0, True)
        sumsq(N_FINAL2, x, xs_u, updated(U_FI2 + 2))

    @block.vector
    def _(dve):
        def conv(p, n=1, i=0):
            for q in range(p, p + n):
                b, half = block_of(q)
                dve.wait_ge(hi_ready, q + 1 + i * 8)
                m = KD * SMALL if q == P_SMALL else PIECE
                dve.tensor_tensor(w_lo[:, q % RING, 0:m], raw[:, b % RAW, half * PIECE:half * PIECE + m],
                                  w_hi[:, q % RING, 0:m], ALU.subtract).then_inc(lo_ready, 1)

        def two(b):
            return bank[b][:].rearrange("p (k n) -> p k n", k=2)

        def mean(n):
            dve.wait_ge(nt["sumsq"], TT * (n + 1))
            dve.tensor_scalar(stat[:, 2:4], stat[:, 0:2], 1.0 / D, EPS, ALU.mult, ALU.add).then_inc(nt["mean"], 1)

        def rows0(n, src, dst):
            dve.wait_ge(nt["rstd"], n + 1)
            dve.tensor_scalar(dst[:, 0, :], src[:, 0, :], stat[:, 4:5], None, ALU.mult).then_inc(nt["rows0"], 1)

        def features(n, f, gain, shift, between=None):
            fi = F_OF[n]
            for g in (1, 3):
                dve.wait_ge(nt["turned"], 4 * fi + g + 1)
                for kk in range(2):
                    kt = 2 * g + kk
                    ps = bank[4 + g][:, kk * SEQ:(kk + 1) * SEQ]
                    if shift is None:
                        last = dve.tensor_scalar(f[:, kt, :], ps, gain[:, kt:kt + 1], None, ALU.mult)
                    else:
                        last = dve.tensor_scalar(f[:, kt, :], ps, gain[:, kt:kt + 1], shift[:, kt:kt + 1],
                                                 ALU.mult, ALU.add)
                last.then_inc(nt["feat_dve"], 1)
            for g in range(4):
                dve.wait_ge(nt["hi"], 4 * fi + g + 1)
                ks = slice(2 * g, 2 * g + 2)
                dve.tensor_tensor(a_lo[:, ks, :], f[:, ks, :], a_hi[:, ks, :], ALU.subtract).then_inc(nt["lo"], 1)
                if between is not None:
                    conv(between + g)

        def features_x(n, gain):
            fi = F_OF[n]
            for g in range(4):
                dve.wait_ge(nt["hi"], 4 * fi + g + 1)
                for kk in range(2):
                    kt = 2 * g + kk
                    last = dve.scalar_tensor_tensor(out=a_lo[:, kt, :], in0=bank[4 + g][:, kk * SEQ:(kk + 1) * SEQ],
                                                    scalar=gain[:, kt:kt + 1], in1=a_hi[:, kt, :],
                                                    op0=ALU.mult, op1=ALU.subtract)
                last.then_inc(nt["lo"], 1)
            mean(n)

        def copy_pair(done, n, dst, b, copied):
            dve.wait_ge(done, n)
            dve.tensor_copy(dst, two(b)).then_inc(copied, 1)

        def ada_ops(k0, slab, slot, i=0, step=0):
            for k in (k0, k0 + 1):
                if k % 4 == 0:
                    dve.wait_ge(ada_landed[k // 4], 16 * (slab + 1) + i * (16 * step))
                w = ada_raw[:, k // 4, (k % 4) * W:(k % 4 + 1) * W]
                c = stat[:, 8 + k:9 + k]
                if k == 0:
                    o = dve.tensor_scalar(slot, w, c, None, ALU.mult)
                else:
                    dve.wait_ge(ada_step, 8 * slab + k + i * (8 * step))
                    o = dve.scalar_tensor_tensor(out=slot, in0=w, scalar=c, in1=slot, op0=ALU.mult, op1=ALU.add)
                o.then_inc(ada_step, 1)

        mean(N_MEM)
        rows0(N_MEM, mem_rows, xs_z)
        dve.wait_ge(sem["vec_turned"], 1)
        dve.tensor_copy(vt[:], bank[7][:, 0:V_ROWS]).then_inc(sem["vec_copied"], 1)
        dve.tensor_copy(taps[:].rearrange("p g k -> p (g k)"), bank[7][:, P:P + CG * TAPS]).then_inc(sem["vec_copied"], 1)
        dve.wait_ge(sem["vec_copied"], 2)
        features(N_MEM, f_z, vt[:, V_MEM:V_MEM + 8], None, P_CKV)
        for s in range(4):
            for k in range(4):
                if s == 0 and k == 0:
                    dve.wait_ge(sem["c_act"], 1)
                ada_ops(2 * k, s, ada_acc[:, s, :])
                if s < 3:
                    conv(P_CKV + 4 * s + 4 + k)
            if s == 3:
                conv(P_SMALL)
            dve.wait_ge(piece_used, P_CKV + 4 * s + 4)
            dst = k_rows if s < 2 else mem_v
            dve.tensor_copy(dst[:, 1, (s % 2) * W:(s % 2 + 1) * W], bank[2 * (s % 2) + 1][:]).then_inc(acc_free[1], 1)
            if s == 0:
                mean(N_H1)
                rows0(N_H1, x, xs_z)
            if s == 2:
                for g in (1, 3):
                    copy_pair(sem["key_turned"], g + 1, mem_kT[:, 2 * g:2 * g + 2, :], 4 + g, sem["key_copied"])
        dve.wait_ge(sem["ada_reduced"], 1)
        dve.tensor_tensor(modT[:, 0:16], bank[4][:, 0:16], vt[:, V_ADA:V_ADA + 16], ALU.add).then_inc(sem["mod_copied"], 1)
        dve.wait_ge(sem["mod_copied"], 1)
        dve.scalar_tensor_tensor(out=gain1[:], in0=modT[:, 8:16], scalar=1.0, in1=vt[:, V_MIX:V_MIX + 8],
                                 op0=ALU.add, op1=ALU.mult).then_inc(sem["gains"], 1)
        dve.wait_ge(sem["gains"], 1)
        features(N_H1, f_z, gain1, modT[:, 0:8])
        conv(P_IN1, 4)
        for s in range(2):
            for k in range(4):
                ada_ops(2 * k, 4 + s, ada_acc[:, s, :])
                conv(P_IN1 + 4 * s + 4 + k)
        with dve.Fori(0, 2) as i:
            for s in range(2):
                for k in range(4):
                    ada_ops(2 * k, 6 + s, ada_acc[:, bass.ds(i * 2 + (2 + s), 1), :].rearrange("p o n -> p (o n)"), i, 2)
                    conv(P_IN1 + 8 + 4 * s + 4 + k, 1, i)

        def project_slabs(p, u, c0, n):
            with dve.Fori(0, n // 2) as i:
                for s in range(2):
                    for k in range(4):
                        conv(p + 4 * s + 4 + k, 1, i)
                    dve.wait_ge(piece_used, p + 4 * s + 4 + i * 8)
                    dve.tensor_scalar(z[:, 1, bass.ds(i * (2 * W) + (c0 + s * W), W)], bank[2 * ((u + s) % 2) + 1][:],
                                      stat[:, 5:6], None, ALU.mult).then_inc(acc_free[1], 1)

        dve.wait_ge(acc_free[0], U_SMALL + 1)
        dve.wait_ge(acc_free[1], U_SMALL + 1)
        for t in range(TT):
            for c in range(2):
                last = dve.tensor_copy(ki2[:, t, c, :], z[:, t, C_KI:C_WI])
        last.then_inc(sem["ki_copied"], 1)
        dve.tensor_scalar(wi_s[:], z[:, :, C_WI:C_U], HEADS ** -0.5, None, ALU.mult).then_inc(sem["wi_scaled"], 1)
        dve.wait_ge(ada_step, 8 * 10)
        dve.memset(conv_in[:, :, 0:PAD], 0.0).then_inc(sem["pad_zeroed"], 1)
        for t in range(TT):
            dve.wait_ge(acc_free[t], U_IN1 + 2)
            dve.tensor_tensor(z[:, t, C_U:C_U + W], z[:, t, C_U:C_U + W], z[:, t, C_U + W:C_U + 2 * W], ALU.mult)\
                .then_inc(sem["glu"], 1)
        copy_pair(sem["t1"], 2, qiT[:, 2:4, :], 5, sem["t1_copied_dve"])
        dve.wait_ge(sem["gate_bias_landed"], 32)

        def gate_rows(n, g, done):
            dve.wait_ge(sem["ada_reduced"], n)
            for c in range(2):
                last = dve.tensor_tensor(g[:, c * W:(c + 1) * W], bank[6 + c][:], g[:, c * W:(c + 1) * W], ALU.add)
            last.then_inc(done, 1)

        def second_modulation():
            gate_rows(2, g_mix, sem["gate_copied"])
            dve.tensor_tensor(modT[:, 24:40], bank[4][:, 0:16], vt[:, V_ADA + 24:V_ADA + 40], ALU.add)\
                .then_inc(sem["mod_copied"], 1)
            dve.wait_ge(sem["mod_copied"], 2)
            dve.scalar_tensor_tensor(out=gain2[:], in0=modT[:, 32:40], scalar=1.0, in1=vt[:, V_FFN:V_FFN + 8],
                                     op0=ALU.add, op1=ALU.mult).then_inc(sem["gains"], 1)

        copy_pair(sem["t1"], 5, qT[:, 2:4, :], 1, sem["t1_copied_dve"])
        dve.wait_ge(sem["conv_turned"], 2)
        dve.tensor_copy(conv_in[:, 2:4, PAD:], two(7)).then_inc(sem["conv_in_dve"], 1)
        dve.wait_ge(sem["wi_scaled"], 1)
        for n in range(TT * HEADS):
            t, h = n // HEADS, n % HEADS
            keys = P * (t + 1)
            dve.wait_ge(sem["relu_done"], n + 1)
            if n:
                dve.wait_ge(sem["score_step"], n)
            add = C("causal", SEQ - keys) if h == 0 else score[:, t, 0:keys]
            dve.scalar_tensor_tensor(out=score[:, t, 0:keys], in0=relu_t[:, n % 2, 0:keys], scalar=wi_s[:, t, h:h + 1],
                                     in1=add, op0=ALU.mult, op1=ALU.add).then_inc(sem["score_step"], 1)
        copy_pair(sem["t1"], 7, kT[:, 2:4, :], 5, sem["t1_copied_dve"])
        dve.wait_ge(sem["conv_in_act"], 1)
        dve.wait_ge(sem["conv_in_dve"], 1)
        taps_done = [0]

        def conv_taps(n):
            for m in range(taps_done[0], min(taps_done[0] + n, CG * TAPS)):
                g, k = m % CG, m // CG
                if k == 0:
                    dve.tensor_scalar(conv_out[:, g, :], conv_in[:, g, 0:SEQ], taps[:, g, 0:1],
                                      vt[:, V_BDW + g:V_BDW + g + 1], ALU.mult, ALU.add).then_inc(sem["conv_done"], 1)
                else:
                    dve.wait_ge(sem["conv_done"], m - CG + 1)
                    dve.scalar_tensor_tensor(out=conv_out[:, g, :], in0=conv_in[:, g, k:k + SEQ], scalar=taps[:, g, k:k + 1],
                                             in1=conv_out[:, g, :], op0=ALU.mult, op1=ALU.add).then_inc(sem["conv_done"], 1)
            taps_done[0] = min(taps_done[0] + n, CG * TAPS)

        step = 0
        for t in range(TT):
            keys = P * (t + 1)
            row = score[:, t, 0:keys]
            dve.wait_ge(sem["score_step"], TT * HEADS)
            for r in range(TOPK // 8):
                if step:
                    dve.wait_ge(sem["top_step"], step)
                dve.max(top8[:], row).then_inc(sem["top_step"], 1)
                conv_taps(1)
                dve.wait_ge(sem["top_step"], step + 1)
                dve.match_replace(row, top8[:], row, TAKEN).then_inc(sem["top_step"], 1)
                conv_taps(1)
                if r % 2:
                    conv(P_IN1 + 28 + 4 * t + r // 2)
                step += 2
            dve.wait_ge(sem["top_step"], step)
            dve.tensor_scalar(row, row, -2e38, -8e30, ALU.is_gt, ALU.mult).then_inc(sem["top_step"], 1)
            dve.wait_ge(sem["top_step"], step + 1)
            dve.tensor_tensor(row, row, C("causal", SEQ - keys), ALU.add).then_inc(sem["top_step"], 1)
            step += 2

        def softmax_steps(tag, bias_of, between=None):
            for n, (h, t) in enumerate(STEPS):
                keys = P * (t + 1)
                bias = bias_of(n, h, t, keys)
                dve.wait_ge(*after(tag, "scores", n + 1))
                if n >= 2:
                    dve.wait_ge(*after(tag, "exp", n - 1))
                dve.tensor_tensor_reduce(s_work[:, n % 2, 0, 0:keys], bank[4 + n % 2][:, 0:keys], bias, DH ** -0.5,
                                         -3e38, ALU.add, ALU.max, stat[:, 32 + n % 2:33 + n % 2])\
                    .then_inc(event(tag, "max"), 1)
                dve.wait_ge(*after(tag, "max", n + 1))
                dve.tensor_scalar(stat[:, 34 + n % 2:35 + n % 2], stat[:, 32 + n % 2:33 + n % 2], -1.0, None, ALU.mult)\
                    .then_inc(event(tag, "negmax"), 1)
                if between is not None:
                    between(n)

        def selected_bias(n, h, t, keys):
            if n:
                dve.wait_ge(*after("a1_", "max", n))
            dve.scalar_tensor_tensor(out=bias_t[:, 0:keys], in0=C("rel", SEQ - keys), scalar=2.0 ** -(h + 1),
                                     in1=score[:, t, 0:keys], op0=ALU.mult, op1=ALU.add).then_inc(event("a1_", "bias"), 1)
            dve.wait_ge(*after("a1_", "bias", n + 1))
            return bias_t[:, 0:keys]

        second_modulation()

        def taps_and_weights(n):
            conv_taps(6)
            if n >= 5 and n % 2:
                conv(P_IN1 + 36 + (n - 5) // 2)

        dve.wait_ge(sem["top_step"], step)
        softmax_steps("a1_", selected_bias, taps_and_weights)
        conv(P_IN1 + 42, 2)
        assert taps_done[0] == CG * TAPS

        def head_outputs(tag, n_steps, heads, banks_of, dst, done):
            dve.wait_ge(*after(tag, "exp", n_steps))
            dve.reciprocal(stat[:, 36:36 + TT * heads], stat[:, 36:36 + TT * heads]).then_inc(event(tag, "recip"), 1)
            dve.wait_ge(*after(tag, "recip", 1))
            dve.wait_ge(*after(tag, "pv", n_steps))
            per = heads // len(banks_of(0))
            for k in range(len(banks_of(0))):
                for t in range(TT):
                    b = banks_of(t)[k]
                    r = stat[:, 36 + t * heads + k * per:36 + t * heads + (k + 1) * per]
                    o = dve.tensor_tensor(dst[:, t, k * W:(k + 1) * W].rearrange("p (h d) -> p h d", h=per),
                                          bank[b][:].rearrange("p (h d) -> p h d", h=per),
                                          r.unsqueeze(2).to_broadcast([P, per, W // per]), ALU.mult)
                    o.then_inc(done, 1)

        head_outputs("a1_", 16, HEADS, lambda t: [t], y_rows, sem["y1"])

        dve.wait_ge(sem["ln_mean"], 1)
        dve.tensor_tensor(conv_out[:], conv_out[:], bank[4][:, 0:SEQ].unsqueeze(1).to_broadcast([P, CG, SEQ]),
                          ALU.subtract).then_inc(sem["ln_centred"], 1)
        dve.wait_ge(sem["ln_centred"], 1)
        dve.tensor_tensor(conv_sq[:], conv_out[:], conv_out[:], ALU.mult).then_inc(sem["ln_square"], 1)
        for g in range(2):
            dve.wait_ge(sem["y1_hi"], g + 1)
            dve.tensor_tensor(a_lo[:, 2 * g:2 * g + 2, :], two(6 + g), a_hi[:, 2 * g:2 * g + 2, :], ALU.subtract)\
                .then_inc(sem["y1_lo"], 1)
        dve.wait_ge(sem["ln_sumsq"], 1)
        dve.tensor_scalar(stat[:, 60:62], bank[5][:, 0:TT], EPS, None, ALU.add).then_inc(sem["ln_var"], 1)
        dve.wait_ge(sem["ln_rstd"], 1)
        for t in range(TT):
            last = dve.tensor_scalar(conv_sq[:, 0, t * P:(t + 1) * P], ident, stat[:, 62 + t:63 + t], None, ALU.mult)
        last.then_inc(sem["ln_diagonal"], 1)

        def gated_first(p1, p2, u, c, c_a):
            conv(p2 + 2 * c, 2)
            dve.wait_ge(piece_used, p1 + 2 * c + 2)
            for t in range(TT):
                dve.tensor_tensor(z[:, t, c * W:(c + 1) * W], bank[2 * ((u + c) % 2) + t][:],
                                  z[:, t, c_a + c * W:c_a + (c + 1) * W], ALU.mult).then_inc(acc_free[t], 1)

        def gated_second(p2, u, c_b, tag):
            for c in range(2):
                conv(p2 + 4 + 2 * c, 2)
                dve.wait_ge(piece_used, p2 + 2 * c + 2)
                for t in range(TT):
                    dve.tensor_tensor(z[:, t, c_b + c * W:c_b + (c + 1) * W], bank[2 * ((u + 2 + c) % 2) + t][:],
                                      z[:, t, c_b + c * W:c_b + (c + 1) * W], ALU.mult).then_inc(acc_free[t], 1)
                    dve.wait_ge(acc_free[t], u + 2 + c + 1)
                    dve.tensor_tensor(z[:, t, c * W:(c + 1) * W], z[:, t, c * W:(c + 1) * W],
                                      z[:, t, c_b + c * W:c_b + (c + 1) * W], ALU.add).then_inc(event(tag, "merged"), 1)

        def merged_lo(tag):
            for g in range(4):
                dve.wait_ge(*after(tag, "hi", g + 1))
                dve.tensor_tensor(a_lo[:, 2 * g:2 * g + 2, :], two(4 + g), a_hi[:, 2 * g:2 * g + 2, :], ALU.subtract)\
                    .then_inc(event(tag, "lo"), 1)

        def residual(t, c, b, gate, done):
            xs, src = x[:, t, c * W:(c + 1) * W], bank[b][:]
            if gate is not None:
                tmp = tmp_rows[:, gated[0] % 2, :]
                dve.tensor_tensor(tmp, src, gate[:, c * W:(c + 1) * W], ALU.mult)\
                    .then_inc(sem["gated"], 1)
                gated[0] += 1
                dve.wait_ge(sem["gated"], gated[0])
                src = tmp
            dve.tensor_tensor(xs, src, xs, ALU.add).then_inc(done, 1)

        gated = [0]

        def project_out(p, u, gate, tag):
            for s in range(2):
                conv(p + 4 * s + 4, 4)
                dve.wait_ge(piece_used, p + 4 * s + 4)
                for t in range(TT):
                    residual(t, s, 2 * ((u + s) % 2) + t, gate, acc_free[t])

        dve.wait_ge(sem["ln_spread"], 1)
        dve.tensor_tensor(conv_out[:], conv_out[:], bank[4][:, 0:SEQ].unsqueeze(1).to_broadcast([P, CG, SEQ]),
                          ALU.mult).then_inc(sem["ln_scaled"], 1)
        dve.wait_ge(sem["conv_hi"], 1)
        dve.tensor_tensor(a_lo[:, 4:8, :], conv_in[:, :, 0:SEQ], a_hi[:, 4:8, :], ALU.subtract).then_inc(sem["conv_lo"], 1)
        for t in range(TT):
            dve.wait_ge(acc_free[t], U_IN1 + 10)
        for c in range(2):
            gated_first(P_PA, P_PC, U_PA, c, C_GA)
        gated_second(P_PC, U_PA, C_GB, "m1_")
        merged_lo("m1_")
        project_out(P_OUT1, U_OUT1, g_mix, "m1_")
        mean(N_H2)
        rows0(N_H2, x, xs_u)
        features(N_H2, f_u, gain2, modT[:, 24:32])

        def feed_forward(p, u, tag, gate, following, ada=None, scaled=False):
            def hidden(s, i=0):
                for t in range(TT):
                    dve.wait_ge(*after(tag, "silu", TT * s + t + 1 + i * 4))
                    up = bank[2 * ((u + s) % 2) + t][:, GW:2 * GW]
                    if scaled:
                        o = dve.scalar_tensor_tensor(out=ff_hid[:, t, :], in0=up, scalar=stat[:, 4 + t:5 + t],
                                                     in1=ff_act[:, t, :], op0=ALU.mult, op1=ALU.mult)
                    else:
                        o = dve.tensor_tensor(ff_hid[:, t, :], up, ff_act[:, t, :], ALU.mult)
                    o.then_inc(event(tag, "hidden"), 1)

            def hidden_lo(s, ks, i=0):
                dve.wait_ge(*after(tag, "hidden_hi", s + 1 + i * 2))
                dve.tensor_tensor(f_lo[:, ks, :], two(4 + s % 2), f_hi[:, ks, :], ALU.subtract)\
                    .then_inc(event(tag, "hidden_lo"), 1)

            conv(p + 4, 4)
            with dve.Fori(0, 5) as i:
                for s in (1, 2):
                    hidden(s - 1, i)
                    conv(p + 4 * s + 4, 2, i)
                    hidden_lo(s - 1, bass.ds(i * 4 + (2 * s - 2), 2), i)
                    conv(p + 4 * s + 6, 2, i)
            last = NSLAB_FF - 1
            hidden(last)
            p += 4 * NSLAB_FF
            conv(p + 4, 2)
            hidden_lo(last, slice(2 * last, 2 * last + 2))
            with dve.Fori(0, 2) as i:
                for k in range(8):
                    conv(p + 6 + k, 1, i)
                    if ada is not None and k % 2:
                        ada_ops(k - 1, ada, ada_acc[:, bass.ds(i + 4, 1), :].rearrange("p o n -> p (o n)"), i, 1)
            conv(p + KF, following)
            if ada is not None:
                gate_rows(3, gate, sem["gate_copied"])
                dve.wait_ge(sem["gate_copied"], 2)
            dve.wait_ge(piece_used, p + KF)
            for t in range(TT):
                for c in range(2):
                    residual(t, c, 2 * t + c, gate, acc_free[t])

        def final_norm(n, landed, done):
            mean(n)
            dve.wait_ge(final_landed, landed)
            dve.wait_ge(nt["rstd"], n + 1)
            for t in range(TT):
                dve.scalar_tensor_tensor(out=x[:, t, :], in0=x[:, t, :], scalar=stat[:, 4 + t:5 + t], in1=final_g[:],
                                         op0=ALU.mult, op1=ALU.mult).then_inc(done, 1)

        feed_forward(P_FI1, U_FI1, "f1_", g_ffn, 4, 10)
        final_norm(N_FINAL1, 16, sem["final1_done"])
        features_x(N_M2, vt[:, V_MIX2:V_MIX2 + 8])
        dve.wait_ge(nt["rstd"], N_M2 + 1)
        project_slabs(P_IN2, U_IN2, 0, 6)

        dve.wait_ge(acc_free[0], U_IN2 + 6)
        dve.wait_ge(acc_free[1], U_IN2 + 6)
        for t in range(TT):
            heads = z[:, t, E_QA:E_VA].rearrange("p (h d) -> p h d", d=DH)
            turned = xs_u[:, t, :].rearrange("p (h d) -> p h d", d=DH)
            cs = C("cos", t * DH, (t + 1) * DH).unsqueeze(1).to_broadcast([P, 16, DH])
            sn_lo = C("sin", t * DH, t * DH + 32).unsqueeze(1).to_broadcast([P, 16, 32])
            sn_hi = C("sin", t * DH + 32, (t + 1) * DH).unsqueeze(1).to_broadcast([P, 16, 32])
            dve.tensor_tensor(turned[:, :, 0:32], heads[:, :, 32:64], sn_lo, ALU.mult)
            dve.tensor_tensor(turned[:, :, 32:64], heads[:, :, 0:32], sn_hi, ALU.mult).then_inc(sem["rope"], 1)
            dve.wait_ge(sem["rope"], t + 1)
            dve.tensor_tensor(heads, heads, cs, ALU.mult).then_inc(sem["rope_cos"], 1)
            dve.wait_ge(sem["rope_cos"], t + 1)
            dve.tensor_tensor(heads, heads, turned, ALU.add).then_inc(sem["rope_sum"], 1)
        copy_pair(sem["t2"], 2, qbT[:, 2:4, :], 5, sem["t2_copied_dve"])
        copy_pair(sem["t2"], 4, kbT[:, 2:4, :], 7, sem["t2_copied_dve"])
        dve.wait_ge(late_landed, 64)
        for c in range(2):
            dve.tensor_tensor_reduce(tmp_rows[:, 0, c * DH:(c + 1) * DH], lam[:, 2 * c, :], lam[:, 2 * c + 1, :], 1.0, 0.0, ALU.mult, ALU.add,
                                     stat[:, 54 + c:55 + c]).then_inc(sem["lam_dots"], 1)
        copy_pair(sem["t2"], 6, qaT[:, 2:4, :], 1, sem["t2_copied_dve"])
        copy_pair(sem["t2"], 8, kaT[:, 2:4, :], 3, sem["t2_copied_dve"])
        dve.wait_ge(sem["lam_exp"], 1)
        dve.scalar_tensor_tensor(out=stat[:, 58:59], in0=stat[:, 56:57], scalar=0.8 - 0.6, in1=stat[:, 57:58],
                                 op0=ALU.add, op1=ALU.subtract).then_inc(sem["lambda"], 1)

        def band_bias(n, h, t, keys):
            if t == 0:
                if n:
                    dve.wait_ge(*after("b_", "max", n))
                dve.scalar_tensor_tensor(out=bias_t[:], in0=rel_rows[:, h, ::-1], scalar=8.0, in1=C("chunk"),
                                         op0=ALU.mult, op1=ALU.add).then_inc(event("b_", "bias"), 1)
                dve.wait_ge(*after("b_", "bias", h + 1))
            return bias_t[:, SEQ - keys:]

        dve.wait_ge(sem["rel_landed"], 16)

        def gate_weights(n):
            if n >= 5 and n % 2:
                conv(P_IN2 + 28 + (n - 5) // 2)

        softmax_steps("b_", band_bias, gate_weights)
        conv(P_IN2 + 34, 2)
        head_outputs("b_", 16, HEADS, lambda t: [t], y2_rows, sem["yb"])
        dve.wait_ge(sem["lambda"], 1)
        for n in range(8):
            h, t = n // 2, n % 2
            keys = P * (t + 1)
            par = n % 2

            def d_mix(m):
                q = m % 2
                ks = P * (m % 2 + 1)
                dve.wait_ge(*after("d_", "exp", 2 * m + 2))
                dve.reciprocal(d_stat[:, 12 + 2 * q:14 + 2 * q], d_stat[:, 8 + 2 * q:10 + 2 * q]).then_inc(event("d_", "recip"), 1)
                dve.wait_ge(*after("d_", "recip", 2 * m + 1))
                dve.tensor_tensor(d_stat[:, 16 + q:17 + q], d_stat[:, 13 + 2 * q:14 + 2 * q], stat[:, 58:59], ALU.mult)\
                    .then_inc(event("d_", "recip"), 1)
                dve.wait_ge(*after("d_", "recip", 2 * m + 2))
                dve.tensor_scalar(p_work[:, q, 1, 0:ks], p_work[:, q, 1, 0:ks], d_stat[:, 16 + q:17 + q], None, ALU.mult)\
                    .then_inc(event("d_", "second"), 1)
                dve.wait_ge(*after("d_", "second", m + 1))
                dve.scalar_tensor_tensor(out=p_work[:, q, 0, 0:ks], in0=p_work[:, q, 0, 0:ks],
                                         scalar=d_stat[:, 12 + 2 * q:13 + 2 * q], in1=p_work[:, q, 1, 0:ks],
                                         op0=ALU.mult, op1=ALU.subtract).then_inc(event("d_", "mix"), 1)

            dve.wait_ge(*after("d_", "scores", n + 1))
            if n >= 2:
                dve.wait_ge(*after("d_", "exp", 2 * (n - 1)))
            for c in range(2):
                dve.tensor_tensor_reduce(s_work[:, par, c, 0:keys], bank[D_BANKS[(2 * n + c) % len(D_BANKS)]][:, 0:keys],
                                         C("chunk", SEQ - keys), DH ** -0.5, -3e38, ALU.add, ALU.max,
                                         d_stat[:, 2 * par + c:2 * par + c + 1]).then_inc(event("d_", "max"), 1)
            dve.wait_ge(*after("d_", "max", 2 * n + 2))
            dve.tensor_scalar(d_stat[:, 4 + 2 * par:6 + 2 * par], d_stat[:, 2 * par:2 * par + 2], -1.0, None, ALU.mult)\
                .then_inc(event("d_", "negmax"), 1)
            if n >= 1:
                d_mix(n - 1)
            if n >= 2:
                conv(P_IN2 + 34 + n)
        d_mix(7)
        conv(P_IN2 + 42, 2)
        dve.wait_ge(*after("d_", "pv", 8))
        for t in range(TT):
            for h in range(4):
                ps = bank[t][:, h * P:(h + 1) * P]
                last = dve.tensor_copy(z[:, t, h * P:(h + 1) * P], ps)
            last.then_inc(sem["ya_rows"], 1)
        dve.wait_ge(sem["ya_rows"], TT)
        for t in range(TT):
            for h in range(4):
                r = z[:, t, h * P:(h + 1) * P]
                last = dve.tensor_tensor_reduce(tmp_rows[:, t, h * P:(h + 1) * P], r, r, 1.0, 0.0, ALU.mult, ALU.add,
                                                d_stat[:, 20 + 4 * t + h:21 + 4 * t + h])
        last.then_inc(sem["ya_sumsq"], 1)
        dve.wait_ge(sem["ya_sumsq"], 1)
        dve.tensor_scalar(stat[:, 16:24], d_stat[:, 20:28], 1.0 / P, EPS, ALU.mult, ALU.add).then_inc(sem["sub_mean"], 1)
        for g in range(2):
            dve.wait_ge(sem["y2_hi"], 1 + g)
            dve.tensor_tensor(a_lo[:, 4 + 2 * g:6 + 2 * g, :], two(6 + g), a_hi[:, 4 + 2 * g:6 + 2 * g, :],
                              ALU.subtract).then_inc(sem["y2_lo"], 1)
        dve.wait_ge(sem["sub_rstd"], 1)
        for t in range(TT):
            r = z[:, t, 0:W].rearrange("p (h d) -> p h d", h=4)
            dve.tensor_tensor(r, r, stat[:, 24 + 4 * t:28 + 4 * t].unsqueeze(2).to_broadcast([P, 4, P]), ALU.mult)\
                .then_inc(sem["ya"], 1)
        for g in range(2):
            dve.wait_ge(sem["y2_turned"], 3 + g)
            dve.tensor_scalar(f_u[:, 2 * g:2 * g + 2, :], two(4 + g), vt[:, V_SUB:V_SUB + 1], 1.0 - (0.8 - 0.6),
                              ALU.mult, ALU.mult).then_inc(sem["ya_feat"], 1)
        for g in range(2):
            dve.wait_ge(sem["y2_hi"], 3 + g)
            dve.tensor_tensor(a_lo[:, 2 * g:2 * g + 2, :], f_u[:, 2 * g:2 * g + 2, :], a_hi[:, 2 * g:2 * g + 2, :],
                              ALU.subtract).then_inc(sem["y2_lo"], 1)
        for t in range(TT):
            dve.wait_ge(acc_free[t], U_IN2 + 10)
        for c in range(2):
            gated_first(P_UB, P_UA, U_UB, c, E_GB)
        gated_second(P_UA, U_UB, E_GA, "m2_")
        merged_lo("m2_")
        project_out(P_OUT2, U_OUT2, None, "m2_")
        features_x(N_CR, vt[:, V_CROSS:V_CROSS + 8])
        dve.wait_ge(nt["rstd"], N_CR + 1)

        for s in range(2):
            conv(P_CQ + 4 + 4 * s, 4)
            dve.wait_ge(piece_used, P_CQ + 4 * s + 4)
            dve.tensor_scalar(qx_rows[:, 1, s * W:(s + 1) * W], bank[2 * ((U_CQ + s) % 2) + 1][:], stat[:, 5:6], None,
                              ALU.mult).then_inc(acc_free[1], 1)
        for g in (1, 3):
            copy_pair(sem["qx_turned"], g + 1, qxT[:, 2 * g:2 * g + 2, :], 4 + g, sem["qx_copied_dve"])
        for n in range(8):
            dve.wait_ge(*after("x_", "scores", n + 1))
            if n >= 2:
                dve.wait_ge(*after("x_", "exp", n - 1))
            dve.tensor_reduce(stat[:, 32 + n % 2:33 + n % 2], bank[4 + n % 2][:, 0:SEQ], AX_X, ALU.max)\
                .then_inc(event("x_", "max"), 1)
            dve.wait_ge(*after("x_", "max", n + 1))
            dve.tensor_scalar(stat[:, 34 + n % 2:35 + n % 2], stat[:, 32 + n % 2:33 + n % 2], -1.0 / 16, None, ALU.mult)\
                .then_inc(event("x_", "negmax"), 1)
        head_outputs("x_", 8, 4, lambda t: [t, 2 + t], merged, event("m3_", "merged"))
        merged_lo("m3_")
        project_out(P_CO, U_CO, None, "m3_")
        features_x(N_F2, vt[:, V_FFN2:V_FFN2 + 8])
        dve.wait_ge(nt["rstd"], N_F2 + 1)
        feed_forward(P_FI2, U_FI2, "f2_", None, 0, scaled=True)
        final_norm(N_FINAL2, 32, sem["result"])

    ctx.close()


_INS = ["x", "c", "norm_mix_g", "w_in", "w_dw", "b_dw", "conv_ln_g", "conv_ln_b", "w_attn_proj", "w_conv_proj", "w_out",
        "norm_ffn_g", "w_ffn_in", "w_ffn_out", "w_ada", "b_ada", "norm_final_g", "mem_2", "norm_mix_g_2", "w_in_2",
        "lam_q1_2", "lam_k1_2", "lam_q2_2", "lam_k2_2", "subln_g_2", "rel_bias_2", "w_up_a_2", "w_up_b_2", "w_out_2",
        "norm_cross_g_2", "norm_mem_g_2", "w_cq_2", "w_ckv_2", "w_co_2", "norm_ffn_g_2", "w_gate_up_2", "w_down_2",
        "norm_final_g_2"]


def kernel(**inputs):
    import numpy as _np
    import concourse.bacc as _bacc
    from concourse.bass_utils import run_bass_kernel_spmd as _run

    nc = _bacc.Bacc("TRN2", target_bir_lowering=False, num_devices=1)
    arrays, args = {}, {}
    for name in _INS:
        v = _np.ascontiguousarray(inputs[name])
        arrays[f"in_{name}"] = v
        args[name] = nc.dram_tensor(f"in_{name}", v.shape, mybir.dt.from_np(v.dtype), kind="ExternalInput").ap()
    out = nc.dram_tensor("out_x", (1, SEQ, D), F32, kind="ExternalOutput").ap()
    build(nc, args, out)
    r = _run(nc, [arrays], core_ids=[0])
    return r.results[0]["out_x"]
```
